# Optimizing a Trainium2 kernel written in Bass

```python
import numpy as np
import jax
import jax.numpy as jnp
from jax import lax

D_MODEL = 1024
BATCH = 1
SEQ = 512
DEPTH = 1

HEAD_DIM = 64
N_HEADS_NSA = 8
N_KV_NSA = 2
G_NSA = N_HEADS_NSA // N_KV_NSA
N_HEADS_SWA = 8
N_KV_SWA = 2
G_SWA = N_HEADS_SWA // N_KV_SWA
D_NSA = N_HEADS_NSA * HEAD_DIM
D_SWA = N_HEADS_SWA * HEAD_DIM
D_MIX = D_NSA + D_SWA
N_HEADS_TOTAL = N_HEADS_NSA + N_HEADS_SWA
KV_NSA = N_KV_NSA * HEAD_DIM
KV_SWA = N_KV_SWA * HEAD_DIM
N_NSA_BRANCHES = 3
IN_SPLITS = (D_NSA,) + (KV_NSA,) * (2 * N_NSA_BRANCHES) + (N_HEADS_NSA * N_NSA_BRANCHES, D_SWA, KV_SWA, KV_SWA)
N_IN = sum(IN_SPLITS)
CMP_LEN = 32
CMP_STRIDE = 16
CMP_HIDDEN = 256
SEL_LEN = 64
SEL_TOPK = 16
SEL_CHUNK = 64
NSA_WINDOW = 512
SWA_WINDOW = 128
BLOCK_Q = 128
N_EXPERTS = 16
N_GROUPS = 4
EXPERTS_PER_GROUP = N_EXPERTS // N_GROUPS
TOP_K = 2
D_EXPERT = 512
EPS = 1e-6
NEG_INF = -1e30
ATTN_SCALE = HEAD_DIM ** -0.5

kernel_name = 'hybrid_nsa_swa_sink_grouped_moe_adaln'

def rms_norm(x, gain):
    xf = x.astype(jnp.float32)
    y = xf * lax.rsqrt(jnp.mean(xf * xf, axis=-1, keepdims=True) + EPS)
    return (y * gain.astype(jnp.float32)).astype(x.dtype)

def alibi_slopes(first, count):
    h = jnp.arange(first + 1, first + count + 1, dtype=jnp.float32)
    return jnp.exp2(-8.0 * h / N_HEADS_TOTAL)

def banded_attention(q, k, v, slopes, window, sinks=None):
    B, T, Hkv, G, Dh = q.shape
    n_blk = T // BLOCK_Q
    span = window + BLOCK_Q
    kp = jnp.pad(k, ((0, 0), (window, 0), (0, 0), (0, 0)))
    vp = jnp.pad(v, ((0, 0), (window, 0), (0, 0), (0, 0)))
    q_b = q.reshape(B, n_blk, BLOCK_Q, Hkv, G, Dh).transpose(1, 0, 2, 3, 4, 5)
    dist = np.arange(BLOCK_Q)[:, None] + window - np.arange(span)[None, :]
    in_band = (dist >= 0) & (dist < window)
    dist_f = jnp.asarray(dist, jnp.float32)

    def one_block(args):
        i, qi = args
        ki = lax.dynamic_slice_in_dim(kp, i * BLOCK_Q, span, axis=1)
        vi = lax.dynamic_slice_in_dim(vp, i * BLOCK_Q, span, axis=1)
        s_abs = i * BLOCK_Q - window + jnp.arange(span)
        mask = in_band & (s_abs >= 0)[None, :]
        s = jnp.einsum('bqhgd,bkhd->bhgqk', qi, ki).astype(jnp.float32)
        s = s - slopes[:, :, None, None] * dist_f
        s = jnp.where(mask, s, NEG_INF)
        if sinks is None:
            p = jax.nn.softmax(s, axis=-1)
        else:
            sink = sinks.astype(jnp.float32)[:, :, None, None]
            m = jnp.maximum(jnp.max(s, axis=-1, keepdims=True), sink)
            e = jnp.exp(s - m)
            p = e / (jnp.sum(e, axis=-1, keepdims=True) + jnp.exp(sink - m))
        return jnp.einsum('bhgqk,bkhd->bqhgd', p.astype(vi.dtype), vi)

    o = lax.map(one_block, (jnp.arange(n_blk), q_b))
    return o.transpose(1, 0, 2, 3, 4, 5).reshape(B, T, Hkv, G, Dh)

def nsa_compressed(q, k, v, pos_k, pos_v, w1k, w2k, w1v, w2v, k_gain, slopes):
    B, T, Hkv, G, Dh = q.shape
    n_cmp = (T - CMP_LEN) // CMP_STRIDE + 1
    idx = np.arange(n_cmp)[:, None] * CMP_STRIDE + np.arange(CMP_LEN)[None, :]

    def compress(z, pos, w1, w2):
        blk = z[:, idx] + pos[None, None, :, None, :]
        blk = blk.transpose(0, 1, 3, 2, 4).reshape(B, n_cmp, Hkv, CMP_LEN * Dh)
        return jax.nn.gelu(blk @ w1) @ w2

    kc = rms_norm(compress(k, pos_k, w1k, w2k), k_gain)
    vc = compress(v, pos_v, w1v, w2v)
    dist = np.arange(T)[:, None] - idx[:, -1][None, :]
    valid = dist >= 0
    s = jnp.einsum('bthgd,bnhd->bthgn', q, kc).astype(jnp.float32)
    s = s - slopes[None, None, :, :, None] * jnp.asarray(dist, jnp.float32)[None, :, None, None, :]
    s = jnp.where(valid[None, :, None, None, :], s, NEG_INF)
    row_valid = jnp.asarray(valid.any(-1), jnp.float32)[None, :, None, None, None]
    p = jax.nn.softmax(s, axis=-1) * row_valid
    o = jnp.einsum('bthgn,bnhd->bthgd', p.astype(vc.dtype), vc)
    return o, p

def nsa_selected(q, k, v, p_cmp, slopes):
    B, T, Hkv, G, Dh = q.shape
    n_cmp = p_cmp.shape[-1]
    n_sel = T // SEL_LEN
    top = min(SEL_TOPK, n_sel)
    cs = np.arange(n_cmp) * CMP_STRIDE
    ss = np.arange(n_sel) * SEL_LEN
    overlap = np.clip(np.minimum(cs[:, None] + CMP_LEN, ss[None, :] + SEL_LEN)
                      - np.maximum(cs[:, None], ss[None, :]), 0, None) / CMP_LEN
    imp = jnp.einsum('bthgn,nj->bthj', p_cmp, jnp.asarray(overlap, jnp.float32))
    cur = np.arange(T) // SEL_LEN
    j = np.arange(n_sel)
    forced = (j[None, :] == 0) | (j[None, :] == cur[:, None]) | (j[None, :] == cur[:, None] - 1)
    future = j[None, :] > cur[:, None]
    imp = jnp.where(forced[None, :, None, :], 1e9, jnp.where(future[None, :, None, :], NEG_INF, imp))
    _, sel = lax.top_k(imp, top)

    k_blocks = k.reshape(B, n_sel, SEL_LEN, Hkv, Dh).transpose(0, 3, 1, 2, 4)
    v_blocks = v.reshape(B, n_sel, SEL_LEN, Hkv, Dh).transpose(0, 3, 1, 2, 4)
    n_chunk = T // SEL_CHUNK
    q_c = q.reshape(B, n_chunk, SEL_CHUNK, Hkv, G, Dh).transpose(1, 0, 3, 2, 4, 5)
    sel_c = sel.reshape(B, n_chunk, SEL_CHUNK, Hkv, top).transpose(1, 0, 3, 2, 4)
    b_ix = jnp.arange(B)[:, None, None, None]
    h_ix = jnp.arange(Hkv)[None, :, None, None]
    within = jnp.arange(SEL_LEN)

    def one_chunk(args):
        ci, qi, si = args
        kg = k_blocks[b_ix, h_ix, si]
        vg = v_blocks[b_ix, h_ix, si]
        t_q = ci * SEL_CHUNK + jnp.arange(SEL_CHUNK)
        s_pos = si[..., None] * SEL_LEN + within
        dist = (t_q[None, None, :, None, None] - s_pos).astype(jnp.float32)[:, :, :, None]
        s = jnp.einsum('bhcgd,bhcnkd->bhcgnk', qi, kg).astype(jnp.float32)
        s = s - slopes[None, :, None, :, None, None] * dist
        s = jnp.where(dist >= 0, s, NEG_INF).reshape(B, Hkv, SEL_CHUNK, G, top * SEL_LEN)
        p = jax.nn.softmax(s, axis=-1)
        vflat = vg.reshape(B, Hkv, SEL_CHUNK, top * SEL_LEN, Dh)
        return jnp.einsum('bhcgm,bhcmd->bhcgd', p.astype(vflat.dtype), vflat)

    o = lax.map(one_chunk, (jnp.arange(n_chunk), q_c, sel_c))
    return o.transpose(1, 0, 3, 2, 4, 5).reshape(B, T, Hkv, G, Dh)

def hybrid_mixer(u, w_in, w_out, q_gain_n, k_gain_n, pos_k, pos_v, w1k, w2k, w1v, w2v,
                 q_gain_s, k_gain_s, sinks, beta_n, beta_s):
    B, T, _ = u.shape
    parts = jnp.split(u @ w_in, np.cumsum(IN_SPLITS)[:-1].tolist(), axis=-1)
    q_n, k_c, v_c, k_sl, v_sl, k_w, v_w, gate_logits, q_s, k_s, v_s = parts

    def kv_n(z):
        return z.reshape(B, T, N_KV_NSA, HEAD_DIM)

    def kv_s(z):
        return z.reshape(B, T, N_KV_SWA, HEAD_DIM)

    slopes_swa = alibi_slopes(0, N_HEADS_SWA).reshape(N_KV_SWA, G_SWA)
    slopes_nsa = alibi_slopes(N_HEADS_SWA, N_HEADS_NSA).reshape(N_KV_NSA, G_NSA)

    q_n = rms_norm(q_n.reshape(B, T, N_KV_NSA, G_NSA, HEAD_DIM), q_gain_n) * ATTN_SCALE
    o_cmp, p_cmp = nsa_compressed(q_n, kv_n(k_c), kv_n(v_c), pos_k, pos_v, w1k, w2k, w1v, w2v,
                                  k_gain_n[0], slopes_nsa)
    o_slc = nsa_selected(q_n, rms_norm(kv_n(k_sl), k_gain_n[1]), kv_n(v_sl), p_cmp, slopes_nsa)
    o_win = banded_attention(q_n, rms_norm(kv_n(k_w), k_gain_n[2]), kv_n(v_w), slopes_nsa, NSA_WINDOW)
    g = jax.nn.sigmoid(gate_logits.reshape(B, T, N_KV_NSA, G_NSA, N_NSA_BRANCHES))
    o_nsa = (g[..., 0:1] * o_cmp + g[..., 1:2] * o_slc + g[..., 2:3] * o_win).reshape(B, T, D_NSA)

    q_s = rms_norm(q_s.reshape(B, T, N_KV_SWA, G_SWA, HEAD_DIM), q_gain_s) * ATTN_SCALE
    o_swa = banded_attention(q_s, rms_norm(kv_s(k_s), k_gain_s), kv_s(v_s), slopes_swa, SWA_WINDOW,
                             sinks.reshape(N_KV_SWA, G_SWA)).reshape(B, T, D_SWA)

    merged = jnp.concatenate([rms_norm(o_nsa, beta_n), rms_norm(o_swa, beta_s)], axis=-1)
    return merged @ w_out

def grouped_moe(u, w_router, w1, w3, w2):
    B, T, D = u.shape
    xt = u.reshape(B * T, D)
    aff = jax.nn.softmax((xt @ w_router).astype(jnp.float32), axis=-1)
    group_score = lax.top_k(aff.reshape(-1, N_GROUPS, EXPERTS_PER_GROUP), TOP_K)[0].sum(-1)
    g_sel = jnp.argmax(group_score, axis=-1)
    in_group = (jnp.arange(N_EXPERTS) // EXPERTS_PER_GROUP)[None, :] == g_sel[:, None]
    top_w, top_i = lax.top_k(jnp.where(in_group, aff, -1.0), TOP_K)
    top_w = top_w / jnp.sum(top_w, axis=-1, keepdims=True)
    gate = jnp.sum(jax.nn.one_hot(top_i, N_EXPERTS, dtype=jnp.float32) * top_w[..., None], axis=1)
    gate = gate.astype(xt.dtype)
    y = jnp.zeros_like(xt)
    for e in range(N_EXPERTS):
        h = jax.nn.silu(xt @ w1[e]) * (xt @ w3[e])
        y = y + gate[:, e:e + 1] * (h @ w2[e])
    return y.reshape(B, T, D)

def setup_inputs(seed: int = 0) -> dict:
    key = jax.random.key(seed)
    ks = jax.random.split(key, 28)
    L = DEPTH

    def nrm(k, shape, scale):
        return jax.random.normal(k, shape, jnp.float32) * scale

    def gain(k, shape):
        return 1.0 + 0.05 * jax.random.normal(k, shape, jnp.float32)

    return {
        'x': nrm(ks[0], (BATCH, SEQ, D_MODEL), 1.0),
        'c': nrm(ks[1], (BATCH, D_MODEL), 1.0),
        'w_router': nrm(ks[2], (D_MODEL, N_EXPERTS), D_MODEL ** -0.5),
        'ada_w': nrm(ks[3], (L, D_MODEL, 6 * D_MODEL), 0.5 * D_MODEL ** -0.5),
        'ada_b': nrm(ks[4], (L, 6 * D_MODEL), 0.01),
        'norm1_g': gain(ks[5], (L, D_MODEL)),
        'norm2_g': gain(ks[6], (L, D_MODEL)),
        'w_in': nrm(ks[7], (L, D_MODEL, N_IN), D_MODEL ** -0.5),
        'w_out': nrm(ks[8], (L, D_MIX, D_MODEL), D_MIX ** -0.5),
        'nsa_q_gain': gain(ks[9], (L, HEAD_DIM)),
        'nsa_k_gain': gain(ks[10], (L, N_NSA_BRANCHES, HEAD_DIM)),
        'cmp_pos_k': nrm(ks[11], (L, CMP_LEN, HEAD_DIM), 0.1),
        'cmp_pos_v': nrm(ks[12], (L, CMP_LEN, HEAD_DIM), 0.1),
        'cmp_w1_k': nrm(ks[13], (L, CMP_LEN * HEAD_DIM, CMP_HIDDEN), (CMP_LEN * HEAD_DIM) ** -0.5),
        'cmp_w2_k': nrm(ks[14], (L, CMP_HIDDEN, HEAD_DIM), CMP_HIDDEN ** -0.5),
        'cmp_w1_v': nrm(ks[15], (L, CMP_LEN * HEAD_DIM, CMP_HIDDEN), (CMP_LEN * HEAD_DIM) ** -0.5),
        'cmp_w2_v': nrm(ks[16], (L, CMP_HIDDEN, HEAD_DIM), CMP_HIDDEN ** -0.5),
        'swa_q_gain': gain(ks[17], (L, HEAD_DIM)),
        'swa_k_gain': gain(ks[18], (L, HEAD_DIM)),
        'swa_sinks': nrm(ks[19], (L, N_HEADS_SWA), 0.5),
        'beta_nsa': gain(ks[20], (L, D_NSA)),
        'beta_swa': gain(ks[21], (L, D_SWA)),
        'moe_w1': nrm(ks[22], (L, N_EXPERTS, D_MODEL, D_EXPERT), D_MODEL ** -0.5),
        'moe_w3': nrm(ks[23], (L, N_EXPERTS, D_MODEL, D_EXPERT), D_MODEL ** -0.5),
        'moe_w2': nrm(ks[24], (L, N_EXPERTS, D_EXPERT, D_MODEL), D_EXPERT ** -0.5),
    }

def reference(x, c, w_router, ada_w, ada_b, norm1_g, norm2_g, w_in, w_out, nsa_q_gain, nsa_k_gain,
              cmp_pos_k, cmp_pos_v, cmp_w1_k, cmp_w2_k, cmp_w1_v, cmp_w2_v, swa_q_gain, swa_k_gain,
              swa_sinks, beta_nsa, beta_swa, moe_w1, moe_w3, moe_w2):
    cond = jax.nn.silu(c)
    for l in range(DEPTH):
        mod = (cond @ ada_w[l] + ada_b[l])[:, None, :]
        sh1, sc1, g1, sh2, sc2, g2 = jnp.split(mod, 6, axis=-1)
        u = rms_norm(x, norm1_g[l]) * (1.0 + sc1) + sh1
        x = x + g1 * hybrid_mixer(u, w_in[l], w_out[l], nsa_q_gain[l], nsa_k_gain[l],
                                  cmp_pos_k[l], cmp_pos_v[l], cmp_w1_k[l], cmp_w2_k[l],
                                  cmp_w1_v[l], cmp_w2_v[l], swa_q_gain[l], swa_k_gain[l],
                                  swa_sinks[l], beta_nsa[l], beta_swa[l])
        u = rms_norm(x, norm2_g[l]) * (1.0 + sc2) + sh2
        x = x + g2 * grouped_moe(u, w_router, moe_w1[l], moe_w3[l], moe_w2[l])
    return x


_drawn_inputs = setup_inputs


def setup_inputs(seed=0):
    import zlib

    import numpy as np

    out = dict(_drawn_inputs(seed))
    spreads = {}
    factors = {'ada_b': 3.165,
     'nsa_q_gain': 4.93,
     'nsa_k_gain': 6.705,
     'cmp_pos_k': 5.502,
     'swa_q_gain': 7.367,
     'swa_k_gain': 3.879,
     'swa_sinks': 25.968,
     'beta_nsa': 3.974,
     'beta_swa': 3.806}
    for name, (base, spread) in spreads.items():
        noise = np.random.default_rng([zlib.crc32(name.encode()), seed]).standard_normal(out[name].shape)
        drawn = base * np.exp(spread * noise) if base else spread * noise
        out[name] = jnp.asarray(drawn.astype(out[name].dtype))
    for name, factor in factors.items():
        out[name] = (out[name] * factor).astype(out[name].dtype)
    return out
```

```python
from contextlib import ExitStack

import concourse.bass as bass
from concourse import mybir

ALU = mybir.AluOpType
ACT = mybir.ActivationFunctionType
AX = mybir.AxisListType
F32 = mybir.dt.float32
BF16 = mybir.dt.bfloat16
I32 = mybir.dt.int32
U32 = mybir.dt.uint32

P = 128
T, D = 512, 1024
TT = T // P
KD = D // P
DH = 64
HN, HS, KV = 8, 8, 2
GQ = HN // KV
AUG = DH + 2
CMP_LEN, CMP_STRIDE, CMP_HID = 32, 16, 256
NC = (T - CMP_LEN) // CMP_STRIDE + 1
SWA_WINDOW = 128
NE, NG, EPG, DE = 16, 4, 4, 512
EPS = 1e-6
NEG = -1e30
C_QN, C_KC, C_VC, C_KSL, C_VSL, C_KW, C_VW, C_GATE, C_QS, C_KS, C_VS = (
    0, 512, 640, 768, 896, 1024, 1152, 1280, 1304, 1816, 1944)
N_IN = 2072
W_GROUPS = [(0, 512), (512, 512), (1024, 280), (1304, 512), (1816, 256)]
R_QN, R_QS, R_KSL, R_KW, R_KS, N_R = 0, 8, 16, 18, 20, 22
MAXB = (2 * T) // P + NE - 1


def decoder_layer(nc, x, c, w_router, ada_w, ada_b, norm1_g, norm2_g, w_in, w_out, nsa_q_gain, nsa_k_gain,
                  cmp_pos_k, cmp_pos_v, cmp_w1_k, cmp_w2_k, cmp_w1_v, cmp_w2_v, swa_q_gain, swa_k_gain,
                  swa_sinks, beta_nsa, beta_swa, moe_w1, moe_w3, moe_w2, out, taps=None):
    slopes_swa = [2.0 ** (-8.0 * (h + 1) / (HN + HS)) for h in range(HS)]
    slopes_nsa = [2.0 ** (-8.0 * (h + 1) / (HN + HS)) for h in range(HS, HN + HS)]

    ctx = ExitStack()
    with ctx:
        def sb(name, shape, dt=F32):
            return ctx.enter_context(nc.sbuf_tensor(name, shape, dt))

        def sem(name):
            return ctx.enter_context(nc.semaphore(name))

        x_sb = sb("x_sb", [P, TT, D])
        norm_x = sb("norm_x", [P, TT, D])
        featT = sb("featT", [P, KD, T])
        ring = sb("ring", [P, 2, 12288])
        w_stage = ring[:, 0, :].rearrange("p (b k n) -> p b k n", b=3, k=KD)
        proj = ring[:, 1, 0:TT * N_IN].rearrange("p (i n) -> p i n", i=TT)
        blk = ring[:, 1, TT * N_IN:TT * N_IN + CMP_LEN * KV * NC].rearrange("p (l m) -> p l m", l=CMP_LEN)
        gate2_row = sb("gate2_row", [P, D])
        gate1_row = sb("gate1_row", [P, D])
        acc = sb("acc", [P, 2, 2048])
        stage = sb("stage", [P, 3, 2048])
        vrow = sb("vrow", [40, P])
        vcol = sb("vcol", [P, 40])
        gain_row = sb("gain_row", [6, AUG])
        gain_col = sb("gain_col", [AUG, 6])
        pos_row = sb("pos_row", [CMP_LEN // 2, 2 * P])
        pos_col = sb("pos_col", [P, CMP_LEN])
        sinks = sb("sinks", [P, HS])
        ident = sb("ident", [P, P])
        identb = sb("identb", [P, P], BF16)
        ones = sb("ones", [P, P])
        minus_half = sb("minus_half", [P, TT * N_R])
        cond = sb("cond", [P, KD])
        cond_e = sb("cond_e", [P, KD])
        mod_col = sb("mod_col", [P, 4 * KD])
        ssq = sb("ssq", [P, TT])
        rstd = sb("rstd", [P, TT])
        sq = acc[:, 0, :]
        junk = stage[:, 0, 0:D]
        hstat = sb("hstat", [P, TT, N_R])
        hrstd = sb("hrstd", [P, TT, N_R])

        att = stage[:, :, :].rearrange("p b n -> p (b n)")

        def view(at, *shape):
            n = 1
            for d in shape:
                n *= d
            v = att[:, at[0]:at[0] + n]
            at[0] += n
            if len(shape) == 2:
                v = v.rearrange("p (a b) -> p a b", a=shape[0])
            if len(shape) == 3:
                v = v.rearrange("p (a b c) -> p a b c", a=shape[0], b=shape[1])
            return v

        at = [0]
        qhat = view(at, 2, TT, AUG)
        qT = view(at, 2, T)
        probs = view(at, 4, T)
        probsT = view(at, 2, T)
        zT = probs
        kchat = view(at, KV, AUG)
        assert at[0] <= 6144
        kT = acc[:, :, :].rearrange("p a n -> p (a n)")[:, 0:6 * T].rearrange("p (a n) -> p a n", a=6)
        acc_rest = acc[:, 1, 1024:2048]
        pcT = acc_rest[:, 0:T]
        kcT = acc_rest[:, T:T + KV * NC].rearrange("p (a n) -> p a n", a=KV)
        vc = acc_rest[:, T + 64:T + 64 + KV * DH].rearrange("p (a n) -> p a n", a=KV)
        kc = acc_rest[:, T + 192:T + 192 + KV * DH].rearrange("p (a n) -> p a n", a=KV)
        hidT = sb("hidT", [P, 4 * KV * NC])
        khat = qhat
        hid = probsT[:, 0, :]
        scr = sb("scr", [P, DH])
        scm = sb("scm", [P, 2, TT, NC])
        ecm = sb("ecm", [P, 2, TT, NC])
        cmax = sb("cmax", [P, 2, TT])
        cfac = sb("cfac", [P, 2, TT])
        zeros_b = sb("zeros_b", [P, 512], BF16)
        squares = norm_x[:, :, :].rearrange("p i (c n) -> p (i c) n", c=2)
        cmpmask = sb("cmpmask", [P, TT, NC])
        causal = sb("causal", [P, P], BF16)
        before = sb("before", [P, P], BF16)
        allmask = sb("allmask", [P, P], BF16)
        tpos = sb("tpos", [P, TT])
        tpos_i = sb("tpos_i", [P, TT], I32)
        cpos = sb("cpos", [P, 1])
        cpos_i = sb("cpos_i", [P, 1], I32)
        augq = sb("augq", [P, HN + HS, TT, 2])
        gates = sb("gates", [P, TT, 3 * HN])
        rowok = sb("rowok", [P, TT])
        nmax = sb("nmax", [P, 4, 2])
        sums = sb("sums", [P, 4, 2])
        fac = sb("fac", [P, 4, 2])
        esink = sb("esink", [P, 4, 2])
        kcss = sb("kcss", [P, 4])
        cmp_w1 = ring[:, 0, 0:CMP_LEN * CMP_HID].rearrange("p (l n) -> p l n", l=CMP_LEN)
        cmp_w2 = ring[:, 0, 8192:8192 + 4 * DH].rearrange("p (a n) -> p a n", a=4)
        w_out_sb = ring[:, 0, 0:KD * D].rearrange("p (k n) -> p k n", k=KD)
        sqf = norm_x[:, :, :].rearrange("p i n -> p (i n)")

        silu = att[:, 0:DE]
        hmid = att[:, DE:2 * DE]
        hT = att[:, 2 * DE:3 * DE].rearrange("p (f n) -> p f n", f=DE // P)
        gsm = att[:, 2048:2048 + (NE + 1) * NE].rearrange("p (e f) -> p e f", e=NE + 1)
        o_tmp = att[:, 3072:4096].rearrange("p (b n) -> p b n", b=2)
        junk2 = att[:, 4096:5120]
        at = [5120]
        aff, first, second, gate, cand, aff2 = [view(at, TT, NE) for _ in range(6)]
        top1, top2, gscore, gsel, gcand = [view(at, TT, NG) for _ in range(5)]
        orstd = view(at, 2 * TT)
        ssq2, rstd2, lmax, lsum, gmax, wsum = [view(at, TT) for _ in range(6)]
        descend = view(at, EPG)
        cmax4 = view(at, TT, NG)
        tri16 = view(at, NE + 1, NE)
        gsf = view(at, NE + 1)
        nb = view(at, NE)
        posf = view(at, 2 * TT)
        wab = view(at, 2 * TT)
        assert at[0] <= 6144
        mcount = sb("mcount", [P, TT * NE], BF16)
        tri_b = sb("tri_b", [P, P], BF16)
        ones_b = sb("ones_b", [P, P], BF16)
        zeros_f = sb("zeros_f", [P, 2 * P])
        idx = sb("idx", [P, 2 * TT], U32)
        block_start = sb("block_start", [1, NE + 1], I32)
        blkbuf = featT[:, :, :].rearrange("p k n -> p (k n)")
        xg = blkbuf[:, 0:D]
        xgT = blkbuf[:, D:2 * D].rearrange("p (k n) -> p k n", k=KD)
        y_sb = blkbuf[:, 2 * D:3 * D]
        yab = ring[:, :, 0:TT * D].rearrange("p b (i n) -> p b i n", i=TT)
        xs = nc.dram_tensor("expert_rows", ((MAXB + 2) * P, D), F32, kind="Internal").ap()
        wr = sb("wr", [P, KD, NE])
        exp_w = [[ring[:, b, m * 4096:(m + 1) * 4096].rearrange("p (k n) -> p k n", k=(KD, KD, DE // P)[m]) for m in range(3)]
                 for b in (1, 0)]

        S2 = [ctx.enter_context(nc.psum_tensor(f"score{i}", [P, 2, 512], F32)) for i in range(2)]
        banks = [S2[0][:, 0, :], S2[0][:, 1, :], S2[1][:, 0, :], S2[1][:, 1, :]]
        banks += [ctx.enter_context(nc.psum_tensor(f"bank{i}", [P, 512], F32))[:, :] for i in range(4, 8)]

        s_small = sem("s_small")
        s_x = sem("s_x")
        s_ada_b = sem("s_ada_b")
        s_ada_b2 = sem("s_ada_b2")
        s_ada_w = [sem(f"s_ada_w{i}") for i in range(3)]
        s_win = [sem(f"s_win{i}") for i in range(3)]
        s_const = sem("s_const")
        s_acc0 = sem("s_acc0")
        s_small_t = sem("s_small_t")
        s_cols = sem("s_cols")
        s_ada_used = sem("s_ada_used")
        s_mod = sem("s_mod")
        s_modc = sem("s_modc")
        s_ssq = sem("s_ssq")
        s_nx = sem("s_nx")
        s_ms = sem("s_ms")
        s_rs = sem("s_rs")
        s_tr = sem("s_tr")
        s_u_a = sem("s_u_a")
        s_u_v = sem("s_u_v")
        s_sinks = sem("s_sinks")
        s_pad = sem("s_pad")
        n_w = sem("n_w")
        n_ew = sem("n_ew")
        n_o = sem("n_o")
        w_w = sem("w_w")
        s_pj = sem("s_pj")
        s_pje_a = sem("s_pje_a")
        s_pje_v = sem("s_pje_v")
        s_act = sem("s_act")
        s_dve = sem("s_dve")
        s_ce = sem("s_ce")
        s_out = sem("s_out")
        s_gp = sem("s_gp")

        s_sq = sem("s_sq")
        s_hred = sem("s_hred")
        s_hms = sem("s_hms")
        s_hrs = sem("s_hrs")
        s_hrs_q = sem("s_hrs_q")
        s_gexp = sem("s_gexp")
        s_khat = sem("s_khat")
        s_kt = sem("s_kt")
        s_kT = sem("s_kT")
        s_zt = sem("s_zt")
        s_zT = sem("s_zT")
        s_blk = sem("s_blk")
        s_hid = sem("s_hid")
        s_gelu = sem("s_gelu")
        s_hidt = sem("s_hidt")
        s_hidT = sem("s_hidT")
        s_kcv = sem("s_kcv")
        s_kcc = sem("s_kcc")
        s_kcsq = sem("s_kcsq")
        s_kcms = sem("s_kcms")
        s_kcrs = sem("s_kcrs")
        s_kchat = sem("s_kchat")
        s_kct = sem("s_kct")
        s_kcT = sem("s_kcT")
        s_cw = sem("s_cw")
        s_wo = sem("s_wo")
        s_mask = sem("s_mask")
        s_poolc = sem("s_poolc")
        n_qhat = sem("n_qhat")
        n_qt = sem("n_qt")
        n_qT = sem("n_qT")
        n_sc = sem("n_sc")
        n_scx = sem("n_scx")
        n_ec = sem("n_ec")
        n_pct = sem("n_pct")
        n_pcT = sem("n_pcT")
        n_s = sem("n_s")
        n_m = sem("n_m")
        n_p = sem("n_p")
        n_pt = sem("n_pt")
        n_pT_v = sem("n_pT_v")
        n_pT_a = sem("n_pT_a")
        n_pv = sem("n_pv")
        w_qhat = sem("w_qhat")
        w_qt = sem("w_qt")
        w_qT = sem("w_qT")
        w_s = sem("w_s")
        w_m = sem("w_m")
        w_p = sem("w_p")
        w_pt = sem("w_pt")
        w_pT_v = sem("w_pT_v")
        w_pT_a = sem("w_pT_a")
        w_pv = sem("w_pv")
        w_o = sem("w_o")
        w_chain = sem("w_chain")
        n_chain = sem("n_chain")

        s_wr = sem("s_wr")
        s_desc = sem("s_desc")
        o_sq = sem("o_sq")
        o_ssq = sem("o_ssq")
        o_ms = sem("o_ms")
        o_rs = sem("o_rs")
        o_pj = sem("o_pj")
        o_a = sem("o_a")
        o_x = sem("o_x")
        r_sq = sem("r_sq")
        r_ms = sem("r_ms")
        r_rs = sem("r_rs")
        r_xh = sem("r_xh")
        r_tr = sem("r_tr")
        r_ev_a = sem("r_ev_a")
        r_ev_v = sem("r_ev_v")
        r_lg = sem("r_lg")
        r_lm = sem("r_lm")
        r_ex = sem("r_ex")
        r_chain = sem("r_chain")
        e_w0 = sem("e_w0")
        e_w1 = sem("e_w1")
        o_fin = sem("o_fin")
        r_cnt = sem("r_cnt")
        r_rank = sem("r_rank")
        t_gs = sem("t_gs")
        t_idx = sem("t_idx")
        t_const = sem("t_const")
        t_zero = sem("t_zero")
        s_rows = sem("s_rows")
        s_scat = sem("s_scat")
        s_xg = sem("s_xg")
        m_h1 = sem("m_h1")
        m_h3 = sem("m_h3")
        m_si = sem("m_si")
        m_h = sem("m_h")
        m_xt = sem("m_xt")
        m_xa = sem("m_xa")
        m_xv = sem("m_xv")
        m_ht = sem("m_ht")
        m_hT = sem("m_hT")
        m_y = sem("m_y")
        m_ye = sem("m_ye")
        c_g = [sem(f"c_g{i}") for i in range(TT)]
        e_w = [e_w0, e_w1]
        out_t = out[0].rearrange("(i p) d -> p i d", p=P)
        x_t = x[0].rearrange("(i p) d -> p i d", p=P)
        ada_t = ada_w[0].rearrange("(k p) n -> k p n", p=P)
        win_t = w_in[0].rearrange("(k p) n -> p k n", p=P)
        def REST(eng, body, last=GQ):
            with eng.Fori(1, last) as i:
                body(i, False)

        KSRC = [(C_KSL, R_KSL, 2), (C_KW, R_KW, 3), (C_KS, R_KS, 5)]
        V_COL = {0: C_VSL, 1: C_VW, 2: C_VS}
        def sq_heads(at0, nh):
            return sqf[:, at0:at0 + TT * nh * DH].rearrange("p (i h d) -> p i h d", i=TT, h=nh)

        block = ctx.enter_context(nc.Block())

        N_ZERO = MAXB + 2

        def blocks_of(eng, e):
            lo = eng.value_load(block_start[0:1, bass.ds(e, 1)], min_val=0, max_val=MAXB)
            hi = eng.value_load(block_start[0:1, bass.ds(e + 1, 1)], min_val=1, max_val=MAXB)
            return lo, hi

        N_SMALL = 16 * (9 + 6)

        @block.sync
        def _(sp):
            sp.dma_start(vrow[0:8, :], c.rearrange("a (r n) -> (a r) n", n=P)).then_inc(s_small, 16)
            sp.dma_start(x_sb[:], x_t).then_inc(s_x, 16)
            sp.dma_start(vrow[8:16, :], norm1_g.rearrange("a (r n) -> (a r) n", n=P)).then_inc(s_small, 16)
            sp.dma_start(vrow[16:24, :], norm2_g.rearrange("a (r n) -> (a r) n", n=P)).then_inc(s_small, 16)
            for b in range(2):
                half = slice(b * GQ * DH, (b + 1) * GQ * DH)
                sp.dma_start(vrow[24:28, b * DH:(b + 1) * DH], beta_nsa[0, half].rearrange("(i d) -> i d", d=DH)).then_inc(s_small, 16)
                sp.dma_start(vrow[28:32, b * DH:(b + 1) * DH], beta_swa[0, half].rearrange("(i d) -> i d", d=DH)).then_inc(s_small, 16)
            for n, pos in enumerate((cmp_pos_k, cmp_pos_v)):
                sp.dma_start(pos_row[:, n * P:(n + 1) * P], pos[0].rearrange("(l b) d -> l (b d)", b=2)).then_inc(s_small, 16)

            def load_ada(n):
                g, k = n // KD, n % KD
                if n >= 3:
                    sp.wait_ge(s_ada_used, n - 2)
                sp.dma_start(stage[:, n % 3, :], ada_t[k, :, g * 2048:(g + 1) * 2048]).then_inc(s_ada_w[n % 3], 16)

            for n in range(3):
                load_ada(n)
            for n in range(3, KD):
                load_ada(n)
            for g, (c0, w) in enumerate(W_GROUPS[:3]):
                if g == 1:
                    sp.wait_ge(s_win[0], 16)
                sp.dma_start(w_stage[:, g, :, 0:w], win_t[:, :, c0:c0 + w]).then_inc(s_win[g], 16)
            for n in range(KD, 3 * KD):
                load_ada(n)

            sp.wait_ge(s_pj, 5 * TT)
            for n, (w1, w2) in enumerate(((cmp_w1_k, cmp_w2_k), (cmp_w1_v, cmp_w2_v))):
                sp.dma_start(cmp_w1[:, n * CMP_LEN // 2:(n + 1) * CMP_LEN // 2, :], w1[0].rearrange("(l p) n -> p l n", p=P)).then_inc(s_cw, 16)
                sp.dma_start(cmp_w2[:, 2 * n:2 * n + 2, :], w2[0].rearrange("(b p) n -> p b n", p=P)).then_inc(s_cw, 16)
            sp.dma_start(wr[:], w_router.rearrange("(k p) n -> p k n", p=P)).then_inc(s_wr, 16)
            sp.wait_ge(t_zero, 1)
            for g in range(N_ZERO):
                sp.dma_start(xs[g * P:(g + 1) * P, :].rearrange("p (a n) -> p a n", n=2 * P),
                             zeros_f[:].unsqueeze(1).broadcast_to([P, D // (2 * P), 2 * P])).then_inc(s_rows, 16)
            sp.wait_ge(s_kcv, 1)
            for g in range(2):
                for b in range(2):
                    rows = w_out[0, g * 512 + b * 256:g * 512 + (b + 1) * 256, :]
                    sp.dma_start(w_out_sb[b * DH:(b + 1) * DH, 4 * g:4 * g + 4, :], rows.rearrange("(i d) n -> d i n", d=DH)).then_inc(s_wo, 16)

            def load_expert(e, b):
                for m, w in enumerate((moe_w1, moe_w3, moe_w2)):
                    sp.dma_start(exp_w[b][m], w[0, bass.ds(e, 1)].rearrange("a (k p) n -> p (a k) n", p=P)).then_inc(e_w[b], 16)

            sp.wait_ge(w_pv, 16)
            load_expert(0, 0)
            sp.wait_ge(o_pj, 2 * TT)
            load_expert(1, 1)
            sp.wait_ge(t_gs, 1)

            def store_outputs(e):
                with sp.Fori(*blocks_of(sp, e)) as g:
                    sp.wait_ge(m_ye, g + 1)
                    sp.dma_start(xs[bass.ds(g * P, P), :], y_sb).then_inc(s_rows, 16)

            with sp.Fori(0, NE // 2 - 1) as n:
                for b in range(2):
                    store_outputs(n * 2 + b)
                    load_expert(n * 2 + (b + 2), b)
            for b in range(2):
                store_outputs(NE - 2 + b)
            for i in range(TT):
                sp.wait_ge(o_fin, i + 1)
                sp.dma_start(out_t[:, i, :], x_sb[:, i, :]).then_inc(s_out, 16)
            sp.wait_ge(s_out, 16 * TT)

        @block.scalar
        def _(act):
            def step(ins):
                step.n += 1
                ins.then_inc(s_act, 1)
                act.wait_ge(s_act, step.n)
            step.n = 0
            gains = [nsa_q_gain[0:1], nsa_k_gain[0, 0:1], nsa_k_gain[0, 1:2], nsa_k_gain[0, 2:3], swa_q_gain[0:1], swa_k_gain[0:1]]
            for n, g in enumerate(gains):
                act.dma_start(gain_row[n:n + 1, 0:DH], g).then_inc(s_small, 16)
            act.dma_start(sinks[:], swa_sinks.broadcast_to([P, HS])).then_inc(s_sinks, 16)
            for g in range(2):
                act.wait_ge(s_acc0, g + 1)
                act.dma_start(acc[0:1, g, :], ada_b[0:1, g * 2048:(g + 1) * 2048]).then_inc(s_ada_b, 16)
            act.wait_ge(s_cols, 1)
            nc.scalar.activation(cond_e[:], vcol[:, 0:8], ACT.Exp, scale=-1.0).then_inc(s_ce, 1)
            act.wait_ge(s_x, 16)
            for i in range(TT):
                nc.scalar.activation(norm_x[:, i, :], x_sb[:, i, :], ACT.Square, accum_out=ssq[:, i:i + 1]).then_inc(s_ssq, 1)
            act.wait_ge(s_modc, 1)
            for k in range(1, KD, 2):
                act.wait_ge(s_tr, k + 1)
                nc.scalar.activation(featT[:, k, :], banks[k % 7][:], ACT.Identity, scale=mod_col[:, k:k + 1],
                                     bias=mod_col[:, 8 + k:9 + k]).then_inc(s_u_a, 1)
            for g, (c0, n) in enumerate(W_GROUPS):
                for i in range(1, TT, 2):
                    act.wait_ge(s_pj, g * TT + i + 1)
                    nc.scalar.activation(proj[:, i, c0:c0 + n], banks[4 + i][:, 0:n], ACT.Copy).then_inc(s_pje_a, 1)
                act.wait_ge(s_pje_v, 2 * (g + 1))
                act.wait_ge(s_pje_a, 2 * (g + 1))
                at0, c1, w1 = [(0, C_QN, 512), (0, C_KSL, 128), (512, C_KW, 128), (2048, C_QS, 512), (1024, C_KS, 128)][g]
                if g == 1:
                    act.wait_ge(s_hred, 1)
                nc.scalar.activation(sqf[:, at0:at0 + TT * w1].rearrange("p (i n) -> p i n", i=TT), proj[:, :, c1:c1 + w1],
                                     ACT.Square).then_inc(s_sq, 1)
                if g + 3 < len(W_GROUPS):
                    act.wait_ge(s_pj, (g + 1) * TT)
                    c1, n1 = W_GROUPS[g + 3]
                    act.dma_start(w_stage[:, g % 3, :, 0:n1], win_t[:, :, c1:c1 + n1]).then_inc(s_win[g % 3], 16)

            nc.scalar.activation(gates[:], proj[:, :, C_GATE:C_GATE + 3 * HN], ACT.Exp, scale=-1.0).then_inc(s_gexp, 1)
            for n in range(4):
                act.wait_ge(s_zt, n + 1)
                nc.scalar.activation(zT[0:DH, n, :], banks[2 + n][0:DH, :], ACT.Copy)
                nc.scalar.activation(zT[DH:P, n, 0:T - 1], banks[2 + n][DH:P, 1:T], ACT.Copy).then_inc(s_zT, 1)
            for n in range(6):
                act.wait_ge(s_kt, n + 1)
                nc.scalar.activation(kT[0:AUG, n, :], banks[n % 2][0:AUG, :], ACT.Copy,
                                     scale=gain_col[:, KSRC[n // 2][2]:KSRC[n // 2][2] + 1]).then_inc(s_kT, 1)
            act.wait_ge(s_hid, 1)
            for n in range(2):
                nc.scalar.activation(hid[0:KV * NC, n * CMP_HID:(n + 1) * CMP_HID], banks[4 + n][0:KV * NC, 0:CMP_HID],
                                     ACT.Gelu_apprx_tanh).then_inc(s_gelu, 1)
            act.wait_ge(s_hidt, 1)
            nc.scalar.activation(hidT[:], banks[6][:, 0:4 * KV * NC], ACT.Copy).then_inc(s_hidT, 1)
            act.wait_ge(s_kcc, 1)
            for v in range(KV):
                nc.scalar.activation(scr[0:NC, :], kc[0:NC, v, :], ACT.Square, accum_out=kcss[0:NC, v:v + 1]).then_inc(s_kcsq, 1)
                act.wait_ge(s_kcsq, v + 1)
            act.wait_ge(s_kct, 1)
            nc.scalar.activation(kcT[0:AUG, :, :], banks[6][0:AUG, 0:KV * NC].rearrange("p (a n) -> p a n", a=KV), ACT.Copy,
                                 scale=gain_col[:, 1:2]).then_inc(s_kcT, 1)

            def queries_T(i, b, qt, qT_sem, gain):
                act.wait_ge(qt, 2 * i + b + 1)
                nc.scalar.activation(qT[0:AUG, b, :], banks[7][0:AUG, :], ACT.Copy, scale=gain_col[:, gain:gain + 1]).then_inc(qT_sem, 1)

            def out_T(i, chunk, beta, sem):
                nc.scalar.activation(squares[:, bass.ds(i + chunk, 1), :].rearrange("p a n -> p (a n)"), banks[6][:], ACT.Square)
                nc.scalar.activation(featT[:, bass.ds(i + chunk, 1), :].rearrange("p a n -> p (a n)"), banks[6][:], ACT.Copy,
                                     scale=vcol[:, bass.ds(i + beta, 1)]).then_inc(sem, 1)

            def pT_out(g, q, fresh):
                w = P * (q + 1)
                act.wait_ge(n_pt, g + 1)
                if not fresh:
                    act.wait_ge(n_pv, g)
                nc.scalar.activation(probsT[:, 1, 0:w], banks[5][:, 0:w], ACT.Copy).then_inc(n_pT_a, 1)

            def nsa(i, first):
                queries_T(i, 0, n_qt, n_qT, 0)
                queries_T(i, 1, n_qt, n_qT, 0)
                for u in range(8):
                    b, q = u % 2, u // 2
                    w = P * (q + 1)
                    if u == 2:
                        act.wait_ge(n_scx, i + 1)
                        nc.scalar.activation(ecm[:], scm[:], ACT.Exp).then_inc(n_ec, 1)
                    if u == 2 and not first:
                        act.wait_ge(n_pv, 8 * i)
                    act.wait_ge(n_m, 8 * i + u + 1)
                    if not (first and u < 2):
                        act.wait_ge(n_pt, 8 * i + u - 1)
                    for r in range(2):
                        ins = nc.scalar.activation(probs[:, 2 * b + r, 0:w], S2[b][:, r, 0:w], ACT.Exp,
                                                   bias=nmax[:, b, r:r + 1], accum_out=sums[:, b, r:r + 1])
                    ins.then_inc(n_p, 1)
                    if u == 2 and not first:
                        out_T(i - 1, 0, 24, n_o)
                    if not (first and u < 2):
                        pT_out(8 * i + u - 2, (u - 2) % 8 // 2, first and u == 2)
                    if u in (5, 6):
                        act.wait_ge(n_pct, 2 * i + u - 4)
                        nc.scalar.activation(pcT[0:NC, :], banks[7][0:NC, :], ACT.Copy).then_inc(n_pcT, 1)

            nsa(0, True)
            REST(act, nsa)
            for g in (30, 31):
                pT_out(g, 3, False)
            act.wait_ge(n_pv, 32)
            out_T(3, 0, 24, n_o)

            def swa_evac(g, fresh):
                act.wait_ge(w_pt, g + 1)
                if not fresh:
                    act.wait_ge(w_pv, g - 1)
                nc.scalar.activation(probsT[:, 1, :], banks[5][:], ACT.Copy).then_inc(w_pT_a, 1)

            def swa(i, first):
                queries_T(i, 0, w_qt, w_qT, 4)
                queries_T(i, 1, w_qt, w_qT, 4)
                for u in range(4):
                    if u == 3 and not first:
                        act.wait_ge(w_pv, 4 * i)
                    act.wait_ge(w_m, 4 * i + u + 1)
                    for q in range(2):
                        nc.scalar.activation(probs[:, u, q * 2 * P:(q + 1) * 2 * P], banks[u][:, q * 2 * P:(q + 1) * 2 * P],
                                                   ACT.Exp, bias=nmax[:, u, q:q + 1], accum_out=sums[:, u, q:q + 1])
                    nc.scalar.activation(esink[:, u, :], nmax[:, u, 0:2], ACT.Exp,
                                         bias=sinks[:, bass.ds(i + GQ * (u % 2), 1)]).then_inc(w_p, 1)
                    if u == 3 and not first:
                        out_T(i - 1, 4, 28, w_o)
                    if u == 3 or (u == 1 and not first):
                        swa_evac(4 * i + u - 2, first)

            swa(0, True)
            REST(act, swa)
            swa_evac(15, False)
            act.wait_ge(w_pv, 16)
            out_T(3, 4, 28, w_o)

            act.wait_ge(o_rs, 1)

            def scaled(j):
                act.wait_ge(o_pj, j + 1)
                if j >= 2:
                    act.wait_ge(o_x, j - 1)
                nc.scalar.activation(o_tmp[:, j % 2, :], banks[2 * (j % 2)], ACT.Copy, scale=orstd[:, j // 2:j // 2 + 1]).then_inc(o_a, 1)

            def squares2(i):
                act.wait_ge(o_x, 2 * i + 2)
                nc.scalar.activation(junk2, x_sb[:, i, :], ACT.Square, accum_out=ssq2[:, i:i + 1]).then_inc(r_sq, 1)
                act.wait_ge(r_sq, i + 1)

            def u2_out(i):
                act.wait_ge(r_tr, i + 1)
                for k in range(4):
                    m = nc.scalar.activation(featT[:, 4 + k, i * P:(i + 1) * P], banks[5 + 2 * (i % 2)][:, k * P:(k + 1) * P],
                                             ACT.Identity, scale=mod_col[:, 20 + k:21 + k], bias=mod_col[:, 28 + k:29 + k])
                m.then_inc(r_ev_a, 1)

            for j in range(2 * TT):
                scaled(j)
                if j % 2 == 1 and j >= 3:
                    squares2((j - 3) // 2)
                if j % 2 == 1 and j >= 5:
                    u2_out((j - 5) // 2)
            squares2(3)
            u2_out(2)
            u2_out(3)
            act.wait_ge(r_lm, 1)
            nc.scalar.activation(aff, aff, ACT.Exp).then_inc(r_ex, 1)

            def xg_load(g):
                act.dma_start(xg, xs[bass.ds(g * P, P), :]).then_inc(s_xg, 16)

            def xg_T(g):
                for k in range(4):
                    m = nc.scalar.activation(xgT[:, 4 + k, :], banks[5][:, k * P:(k + 1) * P], ACT.Identity,
                                             scale=mod_col[:, 20 + k:21 + k], bias=mod_col[:, 28 + k:29 + k])
                m.then_inc(m_xa, 1)

            act.wait_ge(s_scat, 16 * 2 * TT)
            xg_load(0)
            act.wait_ge(m_xt, 1)
            xg_T(0)
            xg_load(1)

            def expert(e):
                with act.Fori(*blocks_of(act, e)) as g:
                    act.wait_ge(m_h1, g + 1)
                    nc.scalar.activation(silu, banks[0], ACT.Silu).then_inc(m_si, 1)
                    for q in range(2):
                        act.wait_ge(m_ht, g * 2 + (q + 1))
                        nc.scalar.activation(hT[:, 2 * q:2 * q + 2, :], banks[6 + q][:, 0:2 * P].rearrange("p (f n) -> p f n", f=2),
                                             ACT.Copy).then_inc(m_hT, 1)
                    act.wait_ge(m_xt, g + 2)
                    xg_T(g + 1)
                    xg_load(g + 2)

            act.wait_ge(t_gs, 1)
            with act.Fori(0, NE) as e:
                expert(e)
            total = act.value_load(block_start[0:1, NE:NE + 1], min_val=NE, max_val=MAXB)
            act.wait_ge(s_xg, total * 16 + 32)
            nc.scalar.activation(ssq2, ssq2, ACT.Copy)

        @block.gpsimd
        def _(pool):
            nc.gpsimd.memset(ident[:], 0.0).then_inc(s_gp, 1)
            nc.gpsimd.memset(acc[:, 0, :], 0.0).then_inc(s_acc0, 1)
            nc.gpsimd.memset(acc[:, 1, :], 0.0).then_inc(s_acc0, 1)
            nc.gpsimd.memset(ones[:], 1.0).then_inc(s_gp, 1)
            nc.gpsimd.memset(gain_row[:, DH:AUG], 1.0).then_inc(s_const, 1)
            nc.gpsimd.memset(minus_half[:], -0.5).then_inc(s_gp, 1)
            pool.wait_ge(s_gp, 3)
            nc.gpsimd.affine_select(out=ident[:], in_=ident[:], compare_op=ALU.not_equal, fill=1.0, base=0,
                                    pattern=[[-1, P]], channel_multiplier=1).then_inc(s_const, 1)
            pool.wait_ge(s_const, 2)
            nc.gpsimd.tensor_copy(identb[:], ident[:]).then_inc(s_const, 1)
            nc.gpsimd.memset(causal[:], 0.0)
            nc.gpsimd.memset(before[:], 0.0)
            nc.gpsimd.memset(allmask[:], NEG)
            nc.gpsimd.memset(cmpmask[:], 0.0)
            nc.gpsimd.memset(rowok[:], 1.0)
            nc.gpsimd.memset(zeros_b[:], 0.0)
            nc.gpsimd.iota(tpos_i[:], pattern=[[P, TT]], base=0, channel_multiplier=1)
            nc.gpsimd.iota(cpos_i[:], pattern=[[0, 1]], base=CMP_LEN - 1, channel_multiplier=CMP_STRIDE).then_inc(s_poolc, 1)
            pool.wait_ge(s_poolc, 1)
            nc.gpsimd.affine_select(out=causal[:], in_=causal[:], compare_op=ALU.is_ge, fill=NEG, base=0,
                                    pattern=[[-1, P]], channel_multiplier=1)
            nc.gpsimd.affine_select(out=before[:], in_=before[:], compare_op=ALU.is_gt, fill=NEG, base=0,
                                    pattern=[[1, P]], channel_multiplier=-1)
            nc.gpsimd.affine_select(out=cmpmask[:], in_=cmpmask[:], compare_op=ALU.is_ge, fill=NEG, base=1 - CMP_LEN,
                                    pattern=[[P, TT], [-CMP_STRIDE, NC]], channel_multiplier=1)
            nc.gpsimd.affine_select(out=rowok[:], in_=rowok[:], compare_op=ALU.is_ge, fill=0.0, base=1 - CMP_LEN,
                                    pattern=[[P, TT]], channel_multiplier=1)
            nc.gpsimd.tensor_copy(tpos[:], tpos_i[:])
            nc.gpsimd.tensor_copy(cpos[:], cpos_i[:]).then_inc(s_poolc, 1)
            pool.wait_ge(s_poolc, 2)
            for h in range(HN + HS):
                slope = (slopes_nsa + slopes_swa)[h]
                nc.gpsimd.memset(augq[:, h, :, 0], slope)
                ins = nc.gpsimd.tensor_scalar(augq[:, h, :, 1], tpos[:], -slope, None, ALU.mult)
            ins.then_inc(s_mask, 1)
            pool.wait_ge(s_ms, 1)
            nc.gpsimd.tensor_tensor(rstd[:], rstd[:], minus_half[:, 0:TT], ALU.pow).then_inc(s_rs, 1)
            pool.wait_ge(s_mod, 1)
            nc.gpsimd.memset(acc[:, 0, :], 0.0).then_inc(s_acc0, 1)
            pool.wait_ge(s_acc0, 3)
            pool.dma_start(acc[0:1, 0, :], ada_b[0:1, 4096:6144]).then_inc(s_ada_b2, 16)
            pool.wait_ge(s_mod, 2)
            nc.gpsimd.memset(pcT[:, :], 0.0)
            nc.gpsimd.memset(vc[:, :, :], 0.0).then_inc(s_pad, 1)
            pool.wait_ge(s_hms, 1)
            for r0, r1, done in ((R_KSL, N_R, s_hrs), (R_QN, R_KSL, s_hrs_q)):
                nc.gpsimd.tensor_tensor(hrstd[:, :, r0:r1], hrstd[:, :, r0:r1],
                                        minus_half[:, 0:TT * (r1 - r0)].rearrange("p (i r) -> p i r", i=TT), ALU.pow).then_inc(done, 1)
            pool.wait_ge(s_kcms, 1)
            nc.gpsimd.tensor_tensor(kcss[0:NC, 0:2], kcss[0:NC, 0:2], minus_half[0:NC, 0:2], ALU.pow).then_inc(s_kcrs, 1)
            for k in range(EPG):
                ins = nc.gpsimd.memset(descend[:, k:k + 1], float(EPG - k))
            ins.then_inc(s_desc, 1)
            nc.gpsimd.memset(zeros_f[:], 0.0).then_inc(t_zero, 1)
            nc.gpsimd.memset(ones_b[:], 1.0)
            nc.gpsimd.memset(tri_b[:], 1.0)
            nc.gpsimd.memset(tri16, 1.0).then_inc(t_const, 1)
            pool.wait_ge(t_const, 1)
            nc.gpsimd.affine_select(out=tri_b[:], in_=tri_b[:], compare_op=ALU.is_gt, fill=0.0, base=0,
                                    pattern=[[1, P]], channel_multiplier=-1)
            nc.gpsimd.affine_select(out=tri16, in_=tri16, compare_op=ALU.is_gt, fill=0.0, base=0,
                                    pattern=[[1, NE + 1], [-1, NE]], channel_multiplier=0).then_inc(t_const, 1)
            pool.wait_ge(o_ms, 1)
            nc.gpsimd.tensor_tensor(orstd, orstd, minus_half[:, 0:2 * TT], ALU.pow).then_inc(o_rs, 1)
            for i in range(TT):
                pool.wait_ge(r_ms, i + 1)
                nc.gpsimd.tensor_tensor(rstd2[:, i:i + 1], rstd2[:, i:i + 1], minus_half[:, 0:1], ALU.pow).then_inc(r_rs, 1)
            pool.wait_ge(s_rows, 16 * N_ZERO)
            pool.wait_ge(t_idx, 1)
            pool.wait_ge(r_xh, TT)
            for n in range(2 * TT):
                pool.indirect_dma_start(out=xs, out_offset=bass.IndirectOffsetOnAxis(ap=idx[:, n:n + 1], axis=0),
                                        in_=norm_x[:, n % TT, :], in_offset=None).then_inc(s_scat, 16)
            total = pool.value_load(block_start[0:1, NE:NE + 1], min_val=NE, max_val=MAXB)
            pool.wait_ge(s_rows, total * 16 + 16 * N_ZERO)
            nc.gpsimd.tensor_tensor(descend, descend, descend, ALU.mult)
            for i in range(TT):
                for b in range(2):
                    pool.indirect_dma_start(out=yab[:, b, i, :], out_offset=None, in_=xs,
                                            in_offset=bass.IndirectOffsetOnAxis(ap=idx[:, b * TT + i:b * TT + i + 1], axis=0)
                                            ).then_inc(c_g[i], 16)

        @block.vector
        def _(dve):
            def step(ins):
                step.n += 1
                ins.then_inc(s_dve, 1)
                dve.wait_ge(s_dve, step.n)
            step.n = 0
            dve.wait_ge(s_small_t, 1)
            nc.vector.tensor_copy(vcol[:, 0:32], banks[0][:, 0:32])
            nc.vector.tensor_copy(gain_col[:], banks[1][0:AUG, 0:6])
            nc.vector.tensor_copy(pos_col[:], banks[2][:, 0:CMP_LEN]).then_inc(s_cols, 1)
            dve.wait_ge(s_ce, 1)
            step(nc.vector.tensor_scalar(cond_e[:], cond_e[:], 1.0, None, ALU.add))
            step(nc.vector.reciprocal(cond_e[:], cond_e[:]))
            step(nc.vector.tensor_tensor(cond[:], cond_e[:], vcol[:, 0:8], ALU.mult))

            def ada(n):
                g, k = n // KD, n % KD
                dve.wait_ge(s_ada_w[n % 3], 16 * (n // 3 + 1))
                if k == 0:
                    if g < 2:
                        dve.wait_ge(s_ada_b, 32)
                    else:
                        dve.wait_ge(s_ada_b2, 16)
                if n > 0:
                    dve.wait_ge(s_ada_used, n)
                nc.vector.scalar_tensor_tensor(out=acc[:, g % 2, :], in0=stage[:, n % 3, :], scalar=cond[:, k:k + 1],
                                               in1=acc[:, g % 2, :], op0=ALU.mult, op1=ALU.add).then_inc(s_ada_used, 1)

            for n in range(2):
                ada(n)
            dve.wait_ge(s_ssq, TT)
            nc.vector.tensor_scalar(rstd[:], ssq[:], 1.0 / D, EPS, ALU.mult, ALU.add).then_inc(s_ms, 1)
            dve.wait_ge(s_rs, 1)
            for i in range(TT):
                nc.vector.tensor_scalar(norm_x[:, i, :], x_sb[:, i, :], rstd[:, i:i + 1], None, ALU.mult).then_inc(s_nx, 1)
            for n in range(2, KD):
                ada(n)
            dve.wait_ge(s_mod, 1)
            nc.vector.scalar_tensor_tensor(out=mod_col[:, 0:8], in0=banks[7][:, 8:16], scalar=1.0, in1=vcol[:, 8:16],
                                           op0=ALU.add, op1=ALU.mult)
            nc.vector.tensor_copy(mod_col[:, 8:16], banks[7][:, 0:8]).then_inc(s_modc, 1)
            dve.wait_ge(s_modc, 1)
            for k in range(0, KD, 2):
                dve.wait_ge(s_tr, k + 1)
                nc.vector.tensor_scalar(featT[:, k, :], banks[k % 7][:], mod_col[:, k:k + 1], mod_col[:, 8 + k:9 + k],
                                        ALU.mult, ALU.add).then_inc(s_u_v, 1)
            n = KD
            for g, (c0, w) in enumerate(W_GROUPS):
                for i in range(0, TT, 2):
                    dve.wait_ge(s_pj, g * TT + i + 1)
                    nc.vector.tensor_copy(proj[:, i, c0:c0 + w], banks[4 + i][:, 0:w]).then_inc(s_pje_v, 1)
                    if i == 0 and g > 0:
                        dve.wait_ge(s_sq, g)
                        at0, r0, nh = [(0, R_QN, 8), (0, R_KSL, 2), (512, R_KW, 2), (2048, R_QS, 8)][g - 1]
                        nc.vector.tensor_reduce(hstat[:, :, r0:r0 + nh], sq_heads(at0, nh), AX.X, ALU.add).then_inc(s_hred, 1)
                    for _ in range(2):
                        if n < 3 * KD:
                            ada(n)
                            n += 1
                            if n == 2 * KD:
                                dve.wait_ge(s_mod, 2)
                                nc.vector.tensor_copy(gate1_row[:, 0:512], banks[0][:])
                                nc.vector.tensor_copy(gate1_row[:, 512:1024], banks[1][:])
                                nc.vector.tensor_copy(mod_col[:, 24:32], banks[2][:, 0:8]).then_inc(s_modc, 1)
                            if n == 3 * KD:
                                dve.wait_ge(s_mod, 3)
                                nc.vector.tensor_copy(gate2_row[:, 0:512], banks[0][:])
                                nc.vector.tensor_copy(gate2_row[:, 512:1024], banks[1][:])
                                nc.vector.scalar_tensor_tensor(
                                    out=mod_col[:, 16:24], in0=banks[2][:, 0:8], scalar=1.0, in1=vcol[:, 16:24],
                                    op0=ALU.add, op1=ALU.mult).then_inc(s_modc, 1)

            dve.wait_ge(s_sq, 5)
            nc.vector.tensor_reduce(hstat[:, :, R_KS:R_KS + 2], sq_heads(1024, 2), AX.X, ALU.add).then_inc(s_hred, 1)
            dve.wait_ge(s_hred, 5)
            nc.vector.tensor_scalar(hrstd[:], hstat[:], 1.0 / DH, EPS, ALU.mult, ALU.add).then_inc(s_hms, 1)
            for b in range(2):
                nc.vector.tensor_copy(khat[:, b, :, DH], tpos[:])
                ins = nc.vector.memset(khat[:, b, :, DH + 1], 1.0)
            nc.vector.tensor_copy(kchat[0:NC, :, DH], cpos[0:NC, 0:1].broadcast_to([NC, KV]))
            nc.vector.memset(kchat[0:NC, :, DH + 1], 1.0)
            dve.wait_ge(s_gexp, 1)
            step(nc.vector.tensor_scalar(gates[:], gates[:], 1.0, None, ALU.add))
            step(nc.vector.reciprocal(gates[:], gates[:]))
            g4 = gates[:].rearrange("p i (h b) -> p i h b", b=3)
            step(nc.vector.tensor_tensor(g4[:, :, :, 0], g4[:, :, :, 0], rowok[:].unsqueeze(2).broadcast_to([P, TT, HN]), ALU.mult))
            dve.wait_ge(s_hrs, 1)
            for n in range(6):
                c0, r0, _ = KSRC[n // 2]
                v = n % 2
                if n >= 2:
                    dve.wait_ge(s_kt, n - 1)
                nc.vector.tensor_tensor(khat[:, n % 2, :, 0:DH], proj[:, :, c0 + v * DH:c0 + (v + 1) * DH],
                                        hrstd[:, :, r0 + v:r0 + v + 1].broadcast_to([P, TT, DH]), ALU.mult).then_inc(s_khat, 1)
            dve.wait_ge(s_zT, 4)
            for n in range(4):
                s2, v = n // KV, n % KV
                for half in range(2):
                    start = half * CMP_STRIDE
                    win = zT[:, n, start:start + NC * CMP_STRIDE].rearrange("p (n l b) -> p l n b", l=CMP_STRIDE // 2, b=2)[:, :, :, 0]
                    l0 = (2 * s2 + half) * CMP_STRIDE // 2
                    ins = nc.vector.tensor_tensor(blk[:, l0:l0 + CMP_STRIDE // 2, v * NC:(v + 1) * NC], win,
                                                  pos_col[:, l0:l0 + CMP_STRIDE // 2].unsqueeze(2).broadcast_to([P, CMP_STRIDE // 2, NC]),
                                                  ALU.add)
            ins.then_inc(s_blk, 1)
            dve.wait_ge(s_kcv, 1)
            b5 = banks[7][0:NC, 0:4 * DH].rearrange("p (a n) -> p a n", a=4)
            nc.vector.tensor_copy(kc[0:NC, :, :], b5[:, 0:2, :])
            dve.wait_ge(s_pad, 1)
            nc.vector.tensor_copy(vc[0:NC, :, :], b5[:, 2:4, :]).then_inc(s_kcc, 1)
            dve.wait_ge(s_kcsq, 2)
            nc.vector.tensor_scalar(kcss[0:NC, 0:2], kcss[0:NC, 0:2], 1.0 / DH, EPS, ALU.mult, ALU.add).then_inc(s_kcms, 1)
            dve.wait_ge(s_kcrs, 1)
            dve.wait_ge(s_kcc, 1)
            for v in range(KV):
                ins = nc.vector.tensor_scalar(kchat[0:NC, v, 0:DH], kc[0:NC, v, :], kcss[0:NC, v:v + 1], None, ALU.mult)
            ins.then_inc(s_kchat, 1)

            def queries(i, b, c0, r0, h0, qhat_sem):
                q = proj[:, :, bass.ds(i * DH + (c0 + b * GQ * DH), DH)]
                nc.vector.scalar_tensor_tensor(out=qhat[:, b, :, 0:DH], in0=q, scalar=DH ** -0.5,
                                               in1=hrstd[:, :, bass.ds(i + (r0 + b * GQ), 1)].broadcast_to([P, TT, DH]),
                                               op0=ALU.mult, op1=ALU.mult)
                nc.vector.tensor_copy(qhat[:, b, :, DH:AUG], augq[:, bass.ds(i + (h0 + b * GQ), 1), :, :].rearrange(
                    "p a i c -> p (a i) c")).then_inc(qhat_sem, 1)

            def chain(ins, sem, base):
                chain.n += 1
                ins.then_inc(sem, 1)
                dve.wait_ge(sem, base + chain.n)

            def gate_cols(i, b, lo, n):
                return gates[:, :, bass.ds(i * 3 + (3 * GQ * b + lo), n)]

            def weigh(i, u, base):
                b, q = u % 2, u // 2
                w = P * (q + 1)
                dve.wait_ge(n_p, 8 * i + u + 1)
                chain(nc.vector.reciprocal(fac[:, b, 0:2], sums[:, b, 0:2]), n_chain, base)
                chain(nc.vector.tensor_tensor(fac[:, b, 0:2], fac[:, b, 0:2], gate_cols(i, b, 1, 2)[:, q, :], ALU.mult), n_chain, base)
                for r in range(2):
                    ins = nc.vector.tensor_scalar(probs[:, 2 * b + r, 0:w], probs[:, 2 * b + r, 0:w], fac[:, b, r:r + 1], None, ALU.mult)
                ins.then_inc(n_w, 1)

            def pT_out(g, q, fresh):
                w = P * (q + 1)
                dve.wait_ge(n_pt, g + 1)
                if not fresh:
                    dve.wait_ge(n_pv, g)
                nc.vector.tensor_copy(probsT[:, 0, 0:w], banks[4][:, 0:w]).then_inc(n_pT_v, 1)

            PER_NSA, PER_SWA = 22, 12

            def nsa(i, first, next_queries):
                chain.n = 0
                base = PER_NSA * i
                for u in range(8):
                    b, q = u % 2, u // 2
                    w = P * (q + 1)
                    if u == 2:
                        dve.wait_ge(n_sc, i + 1)
                        for c2 in range(2):
                            b7 = banks[7][:, c2 * P:c2 * P + TT * NC].rearrange("p (i n) -> p i n", i=TT)
                            chain(nc.vector.tensor_tensor(scm[:, c2], b7, cmpmask[:], ALU.add), n_chain, base)
                        chain(nc.vector.tensor_reduce(cmax[:], scm[:], AX.X, ALU.max, negate=True), n_chain, base)
                        nc.vector.tensor_tensor(scm[:].rearrange("p b i n -> p (b i) n"), scm[:].rearrange("p b i n -> p (b i) n"),
                                                cmax[:].rearrange("p b i -> p (b i)").unsqueeze(2).broadcast_to([P, 2 * TT, NC]),
                                                ALU.add).then_inc(n_scx, 1)
                    dve.wait_ge(n_s, 8 * i + u + 1)
                    nc.vector.tensor_reduce(nmax[:, b, 0:2], S2[b][:, :, 0:w], AX.X, ALU.max, negate=True).then_inc(n_m, 1)
                    if u == 6:
                        next_queries()
                    if u > 0:
                        weigh(i, u - 1, base)
                    if not (first and u < 2):
                        pT_out(8 * i + u - 2, (u - 2) % 8 // 2, first and u == 2)
                    if u == 4:
                        dve.wait_ge(n_ec, i + 1)
                        chain(nc.vector.tensor_reduce(cfac[:], ecm[:], AX.X, ALU.add), n_chain, base)
                        chain(nc.vector.reciprocal(cfac[:], cfac[:]), n_chain, base)
                        for c2 in range(2):
                            ins = nc.vector.tensor_tensor(cfac[:, c2, :], cfac[:, c2, :], gate_cols(i, c2, 0, 1).rearrange(
                                "p i a -> p (i a)"), ALU.mult)
                        chain(ins, n_chain, base)
                        nc.vector.tensor_tensor(ecm[:].rearrange("p b i n -> p (b i) n"), ecm[:].rearrange("p b i n -> p (b i) n"),
                                                cfac[:].rearrange("p b i -> p (b i)").unsqueeze(2).broadcast_to([P, 2 * TT, NC]),
                                                ALU.mult).then_inc(n_ew, 1)
                weigh(i, 7, base)
                assert chain.n == PER_NSA, chain.n

            dve.wait_ge(s_kt, 6)
            dve.wait_ge(s_mask, 1)
            dve.wait_ge(s_hrs_q, 1)
            for b in range(2):
                queries(0, b, C_QN, R_QN, 0, n_qhat)

            def nsa_then_queries(i, first):
                nsa(i, first, lambda: [queries(i + 1, b, C_QN, R_QN, 0, n_qhat) for b in range(2)])

            nsa_then_queries(0, True)
            REST(dve, nsa_then_queries, GQ - 1)
            nsa(GQ - 1, False, lambda: [queries(0, b, C_QS, R_QS, HN, w_qhat) for b in range(2)])
            for g in (30, 31):
                pT_out(g, 3, False)

            def swa_weigh(i, u, base):
                dve.wait_ge(w_p, 4 * i + u + 1)
                chain(nc.vector.tensor_tensor(fac[:, u, 0:2], sums[:, u, 0:2], esink[:, u, :], ALU.add), w_chain, base)
                chain(nc.vector.reciprocal(fac[:, u, 0:2], fac[:, u, 0:2]), w_chain, base)
                for q in range(2):
                    ins = nc.vector.tensor_scalar(probs[:, u, q * 2 * P:(q + 1) * 2 * P], probs[:, u, q * 2 * P:(q + 1) * 2 * P],
                                                  fac[:, u, q:q + 1], None, ALU.mult)
                ins.then_inc(w_w, 1)

            def swa_evac(g, u, fresh):
                dve.wait_ge(w_pt, g + 1)
                if not fresh:
                    dve.wait_ge(w_pv, g - 1)
                lo = P if u < 2 else 0
                nc.vector.tensor_copy(probsT[:, 0, lo:512], banks[4][:, lo:512]).then_inc(w_pT_v, 1)

            def swa(i, first, next_queries):
                chain.n = 0
                base = PER_SWA * i
                for u in range(4):
                    b = u % 2
                    dve.wait_ge(w_s, 4 * i + u + 1)
                    chain(nc.vector.tensor_reduce(nmax[:, u, 0:2], banks[u][:].rearrange("p (q n) -> p q n", q=2), AX.X, ALU.max),
                          w_chain, base)
                    nc.vector.tensor_scalar(nmax[:, u, 0:2], nmax[:, u, 0:2], sinks[:, bass.ds(i + GQ * b, 1)], -1.0,
                                            ALU.max, ALU.mult).then_inc(w_m, 1)
                    if u == 2:
                        next_queries()
                    if u > 0:
                        swa_weigh(i, u - 1, base)
                    if u == 2 or (u == 0 and not first):
                        swa_evac(4 * i + u - 2, (u - 2) % 4, first)
                swa_weigh(i, 3, base)
                assert chain.n == PER_SWA

            def swa_then_queries(i, first):
                swa(i, first, lambda: [queries(i + 1, b, C_QS, R_QS, HN, w_qhat) for b in range(2)])

            dve.wait_ge(s_sinks, 16)
            swa_then_queries(0, True)
            dve.wait_ge(n_o, GQ)
            for n in range(1, 4):
                nc.vector.tensor_tensor(squares[:, 0, :], squares[:, 0, :], squares[:, n, :], ALU.add).then_inc(o_sq, 1)
                dve.wait_ge(o_sq, n)
            REST(dve, swa_then_queries, GQ - 1)
            swa(GQ - 1, False, lambda: None)
            swa_evac(14, 2, False)

            for n in range(1, 4):
                dve.wait_ge(w_o, n + 1)
                nc.vector.tensor_tensor(squares[:, 4, :], squares[:, 4, :], squares[:, 4 + n, :], ALU.add).then_inc(o_sq, 1)
                dve.wait_ge(o_sq, n + 3)
            dve.wait_ge(o_ssq, 1)
            nc.vector.tensor_scalar(orstd, banks[7][:, 0:2 * TT], 1.0 / 512, EPS, ALU.mult, ALU.add).then_inc(o_ms, 1)
            dve.wait_ge(o_rs, 1)
            chain.n = 0

            def residual1(j):
                i, h = j // 2, slice((j % 2) * 512, (j % 2 + 1) * 512)
                dve.wait_ge(o_a, j + 1)
                t = o_tmp[:, j % 2, :]
                chain(nc.vector.scalar_tensor_tensor(out=t, in0=banks[2 * (j % 2) + 1], scalar=orstd[:, TT + i:TT + i + 1], in1=t,
                                                     op0=ALU.mult, op1=ALU.add), r_chain, 0)
                chain(nc.vector.tensor_tensor(t, t, gate1_row[:, h], ALU.mult), r_chain, 0)
                nc.vector.tensor_tensor(x_sb[:, i, h], x_sb[:, i, h], t, ALU.add).then_inc(o_x, 1)

            def norm2(i):
                dve.wait_ge(r_sq, i + 1)
                nc.vector.tensor_scalar(rstd2[:, i:i + 1], ssq2[:, i:i + 1], 1.0 / D, EPS, ALU.mult, ALU.add).then_inc(r_ms, 1)
                dve.wait_ge(r_rs, i + 1)
                dve.wait_ge(o_x, 2 * i + 2)
                nc.vector.tensor_scalar(norm_x[:, i, :], x_sb[:, i, :], rstd2[:, i:i + 1], None, ALU.mult).then_inc(r_xh, 1)

            def u2_out(i):
                dve.wait_ge(r_tr, i + 1)
                for k in range(4):
                    m = nc.vector.tensor_scalar(featT[:, k, i * P:(i + 1) * P], banks[4 + 2 * (i % 2)][:, k * P:(k + 1) * P],
                                                mod_col[:, 16 + k:17 + k], mod_col[:, 24 + k:25 + k], ALU.mult, ALU.add)
                m.then_inc(r_ev_v, 1)

            for j in range(2 * TT):
                residual1(j)
                if j % 2 == 1 and j >= 3:
                    norm2((j - 3) // 2)
                if j % 2 == 1 and j >= 5:
                    u2_out((j - 5) // 2)
            norm2(3)
            u2_out(2)
            u2_out(3)

            def ch(ins):
                chain(ins, r_chain, 0)

            def g4(v):
                return v.rearrange("p i (g e) -> p (i g) e", e=EPG)

            def flat(v):
                return v.rearrange("p i g -> p (i g)")

            def over(v, n):
                return v.unsqueeze(2).broadcast_to([P, v.shape[1], n])

            dve.wait_ge(r_lg, TT)
            dve.wait_ge(s_desc, 1)
            lg = banks[0][:, 0:TT * NE].rearrange("p (i e) -> p i e", i=TT)
            ch(nc.vector.tensor_reduce(lmax, lg, AX.X, ALU.max, negate=True))
            nc.vector.tensor_tensor(aff, lg, over(lmax, NE), ALU.add).then_inc(r_lm, 1)
            dve.wait_ge(r_ex, 1)
            ch(nc.vector.tensor_reduce(lsum, aff, AX.X, ALU.add))
            ch(nc.vector.reciprocal(lsum, lsum))
            ch(nc.vector.tensor_tensor(aff, aff, over(lsum, NE), ALU.mult))

            def first_max(onehot, scores, best, work, count):
                ch(nc.vector.tensor_reduce(best, scores, AX.X, ALU.max))
                ch(nc.vector.tensor_tensor(work, scores, over(best, EPG), ALU.is_equal))
                ch(nc.vector.tensor_tensor(work, work, descend.unsqueeze(1).broadcast_to([P, count, EPG]), ALU.mult))
                ch(nc.vector.tensor_reduce(flat(cmax4)[:, 0:count], work, AX.X, ALU.max))
                ch(nc.vector.tensor_tensor(onehot, work, over(flat(cmax4)[:, 0:count], EPG), ALU.is_equal))

            first_max(g4(first), g4(aff), flat(top1), g4(cand), TT * NG)
            ch(nc.vector.scalar_tensor_tensor(out=aff2, in0=first, scalar=-4.0, in1=aff, op0=ALU.mult, op1=ALU.add))
            first_max(g4(second), g4(aff2), flat(top2), g4(cand), TT * NG)
            ch(nc.vector.tensor_tensor(gscore, top1, top2, ALU.add))
            first_max(gsel, gscore, gmax, gcand, TT)
            ch(nc.vector.tensor_tensor(g4(first), g4(first), over(flat(gsel), EPG), ALU.mult))
            ch(nc.vector.tensor_tensor(g4(second), g4(second), over(flat(gsel), EPG), ALU.mult))
            nc.vector.tensor_tensor(mcount[:], flat(first), flat(second), ALU.add).then_inc(r_cnt, 1)
            dve.wait_ge(r_rank, 1)
            dve.wait_ge(t_const, 2)
            tot = banks[1][:, TT * NE:TT * NE + NE]
            ch(nc.vector.tensor_scalar(nb, tot, float(P), 1.0, ALU.is_gt, ALU.add))
            for m in (2, 3):
                ch(nc.vector.scalar_tensor_tensor(out=nb, in0=tot, scalar=float(m * P), in1=nb, op0=ALU.is_gt, op1=ALU.add))
            ch(nc.vector.tensor_tensor(gsm, tri16, nb.unsqueeze(1).broadcast_to([P, NE + 1, NE]), ALU.mult))
            ch(nc.vector.tensor_reduce(gsf, gsm, AX.X, ALU.add))
            nc.vector.tensor_copy(block_start[:], gsf[0:1, :]).then_inc(t_gs, 1)
            ch(nc.vector.scalar_tensor_tensor(out=aff2, in0=gsf[:, 0:NE].unsqueeze(1).broadcast_to([P, TT, NE]), scalar=float(P),
                                              in1=banks[1][:, 0:TT * NE].rearrange("p (i e) -> p i e", i=TT), op0=ALU.mult, op1=ALU.add))
            for b, t in enumerate((first, second)):
                ch(nc.vector.tensor_tensor(t, t, aff2, ALU.mult))
                ch(nc.vector.tensor_reduce(posf[:, b * TT:(b + 1) * TT], t, AX.X, ALU.add))
            nc.vector.tensor_copy(idx[:], posf).then_inc(t_idx, 1)
            for b, t in enumerate((top1, top2)):
                ch(nc.vector.tensor_tensor(t, t, gsel, ALU.mult))
                ch(nc.vector.tensor_reduce(wab[:, b * TT:(b + 1) * TT], t, AX.X, ALU.add))
            ch(nc.vector.tensor_tensor(wsum, wab[:, 0:TT], wab[:, TT:2 * TT], ALU.add))
            ch(nc.vector.reciprocal(wsum, wsum))
            for b in range(2):
                ch(nc.vector.tensor_tensor(wab[:, b * TT:(b + 1) * TT], wab[:, b * TT:(b + 1) * TT], wsum, ALU.mult))

            def xg_T(g):
                dve.wait_ge(m_xt, g + 1)
                for k in range(4):
                    m = nc.vector.tensor_scalar(xgT[:, k, :], banks[4][:, k * P:(k + 1) * P], mod_col[:, 16 + k:17 + k],
                                                mod_col[:, 24 + k:25 + k], ALU.mult, ALU.add)
                m.then_inc(m_xv, 1)

            def expert(e):
                with dve.Fori(*blocks_of(dve, e)) as g:
                    dve.wait_ge(m_h3, g + 1)
                    dve.wait_ge(m_si, g + 1)
                    for q in range(2):
                        h = slice(q * DE // 2, (q + 1) * DE // 2)
                        nc.vector.tensor_tensor(hmid[:, h], silu[:, h], banks[1][:, h], ALU.mult).then_inc(m_h, 1)
                    xg_T(g + 1)
                    dve.wait_ge(s_rows, g * 16 + 16 * N_ZERO)
                    for n in range(2):
                        dve.wait_ge(m_y, g * 2 + (n + 1))
                        m = nc.vector.tensor_tensor(y_sb[:, n * 512:(n + 1) * 512], banks[2 + n], gate2_row[:, n * 512:(n + 1) * 512], ALU.mult)
                    m.then_inc(m_ye, 1)

            xg_T(0)
            dve.wait_ge(t_gs, 1)
            with dve.Fori(0, NE) as e:
                expert(e)
            for i in range(TT):
                dve.wait_ge(c_g[i], 32)
                ch(nc.vector.scalar_tensor_tensor(out=x_sb[:, i, :], in0=yab[:, 0, i, :], scalar=wab[:, i:i + 1], in1=x_sb[:, i, :],
                                                  op0=ALU.mult, op1=ALU.add))
                nc.vector.scalar_tensor_tensor(out=x_sb[:, i, :], in0=yab[:, 1, i, :], scalar=wab[:, TT + i:TT + i + 1],
                                               in1=x_sb[:, i, :], op0=ALU.mult, op1=ALU.add).then_inc(o_fin, 1)

        @block.tensor
        def _(pe):
            pe.wait_ge(s_const, 3)
            pe.wait_ge(s_small, N_SMALL)
            nc.tensor.transpose(banks[0][:, 0:32], vrow[0:32, :], ident[0:32, 0:32])
            nc.tensor.transpose(banks[1][0:AUG, 0:6], gain_row[:, :], ident[0:6, 0:6])
            for n in range(2):
                h = CMP_LEN // 2
                m = nc.tensor.transpose(banks[2][:, n * h:(n + 1) * h], pos_row[:, n * P:(n + 1) * P], ident[0:h, 0:h])
            m.then_inc(s_small_t, 1)
            pe.wait_ge(s_cols, 1)
            pe.wait_ge(s_nx, TT)

            def x_transposes(k):
                if k == KD - 1:
                    pe.wait_ge(s_u_v, 1)
                for i in range(TT):
                    m = nc.tensor.transpose(banks[k % 7][:, i * P:(i + 1) * P], norm_x[:, i, k * P:(k + 1) * P], ident[:])
                m.then_inc(s_tr, 1)

            for k in range(KD - 1):
                x_transposes(k)
            pe.wait_ge(s_ada_used, KD)
            for k in range(16):
                m = nc.tensor.matmul(banks[7][:, k:k + 1], acc[:, 0, k * P:(k + 1) * P], ones[:, 0:1], start=True, stop=True)
            m.then_inc(s_mod, 1)
            x_transposes(KD - 1)
            pe.wait_ge(s_u_v, KD // 2)
            pe.wait_ge(s_u_a, KD // 2)

            def project(g, i):
                c0, n = W_GROUPS[g]
                if i == 0:
                    pe.wait_ge(s_win[g % 3], 16 * (g // 3 + 1))
                if g > 0:
                    pe.wait_ge(s_pje_v if i % 2 == 0 else s_pje_a, 2 * (g - 1) + i // 2 + 1)
                elif i == 3:
                    pe.wait_ge(s_modc, 1)
                for k in range(KD):
                    m = nc.tensor.matmul(banks[4 + i][:, 0:n], featT[:, k, i * P:(i + 1) * P], w_stage[:, g % 3, k, 0:n],
                                         start=(k == 0), stop=(k == KD - 1))
                m.then_inc(s_pj, 1)

            for g in range(len(W_GROUPS)):
                for i in range(TT):
                    project(g, i)
                if g in (2, 4):
                    b = 1 if g == 2 else 0
                    pe.wait_ge(s_ada_used, 16 if g == 2 else 24)
                    if g == 4:
                        pe.wait_ge(s_modc, 2)
                    row, col = (0, 1024) if g == 2 else (1024, 0)
                    for h in range(2):
                        nc.tensor.matmul(banks[h][:], ones[:], acc[:, b, row + h * 512:row + (h + 1) * 512], start=True, stop=True)
                    for k in range(8):
                        m = nc.tensor.matmul(banks[2][:, k:k + 1], acc[:, b, col + k * P:col + (k + 1) * P], ones[:, 0:1],
                                             start=True, stop=True)
                    m.then_inc(s_mod, 1)

            pe.wait_ge(s_modc, 3)
            pe.wait_ge(s_pje_v, 10)
            pe.wait_ge(s_pje_a, 10)
            for n in range(4):
                for i in range(TT):
                    z = proj[:, i, C_KC + n * DH:C_KC + (n + 1) * DH]
                    nc.tensor.transpose(banks[2 + n][0:DH, i * P:(i + 1) * P], z, ident[:])
                    m = nc.tensor.matmul(banks[2 + n][DH:P, i * P:(i + 1) * P], z, ident[:], start=True, stop=True)
                m.then_inc(s_zt, 1)
            for n in range(6):
                pe.wait_ge(s_khat, n + 1)
                if n >= 2:
                    pe.wait_ge(s_kT, n - 1)
                for i in range(TT):
                    m = nc.tensor.transpose(banks[n % 2][0:AUG, i * P:(i + 1) * P], khat[:, n % 2, i, :], ident[:])
                m.then_inc(s_kt, 1)
            pe.wait_ge(s_blk, 1)
            pe.wait_ge(s_cw, 64)
            for s2 in range(2):
                for l in range(CMP_LEN // 2):
                    m = nc.tensor.matmul(banks[4 + s2][0:KV * NC, 0:CMP_HID], blk[:, s2 * CMP_LEN // 2 + l, :],
                                         cmp_w1[:, s2 * CMP_LEN // 2 + l, :], start=(l == 0), stop=(l == CMP_LEN // 2 - 1))
            m.then_inc(s_hid, 1)
            pe.wait_ge(s_gelu, 2)
            for n in range(4):
                m = nc.tensor.transpose(banks[6][:, n * KV * NC:(n + 1) * KV * NC], hid[0:KV * NC, n * P:(n + 1) * P],
                                        ident[0:KV * NC, 0:KV * NC])
            m.then_inc(s_hidt, 1)
            pe.wait_ge(s_hidT, 1)
            for s2 in range(2):
                for v in range(KV):
                    for hb in range(2):
                        o = (2 * s2 + hb) * KV * NC + v * NC
                        m = nc.tensor.matmul(banks[7][0:NC, (2 * s2 + v) * DH:(2 * s2 + v + 1) * DH], hidT[:, o:o + NC],
                                             cmp_w2[:, 2 * s2 + hb, :], start=(hb == 0), stop=(hb == 1))
            m.then_inc(s_kcv, 1)
            pe.wait_ge(s_kchat, 1)
            for v in range(KV):
                m = nc.tensor.transpose(banks[6][0:AUG, v * NC:(v + 1) * NC], kchat[0:NC, v, :], ident[0:NC, 0:NC])
            m.then_inc(s_kct, 1)
            pe.wait_ge(s_kcT, 1)
            pe.wait_ge(s_mask, 1)

            def queries_T(i, b, qhat_sem, qT_sem, qt):
                pe.wait_ge(qhat_sem, 2 * i + b + 1)
                if b == 1:
                    pe.wait_ge(qT_sem, 2 * i + 1)
                for k in range(TT):
                    m = nc.tensor.transpose(banks[7][0:AUG, k * P:(k + 1) * P], qhat[:, b, k, :], ident[:])
                m.then_inc(qt, 1)

            def clear_out(o_sem, i, first):
                if not first:
                    pe.wait_ge(o_sem, i)
                for b in range(2):
                    nc.tensor.matmul(banks[6][b * DH:(b + 1) * DH, :], zeros_b[:, 0:DH], zeros_b[:], start=True, stop=False,
                                     skip_group_check=True)

            def nsa_T(g, q, b, fresh):
                pe.wait_ge(n_w, g + 1)
                if not fresh:
                    pe.wait_ge(n_pT_v, g)
                    pe.wait_ge(n_pT_a, g)
                for r in range(2):
                    for k in range(q + 1):
                        m = nc.tensor.transpose(banks[4 + r][:, k * P:(k + 1) * P], probs[:, 2 * b + r, k * P:(k + 1) * P], ident[:])
                m.then_inc(n_pt, 1)

            def nsa_PV(g, q, b):
                pe.wait_ge(n_pT_v, g + 1)
                pe.wait_ge(n_pT_a, g + 1)
                for r in range(2):
                    for k in range(q + 1):
                        m = nc.tensor.matmul(banks[6][b * DH:(b + 1) * DH, q * P:(q + 1) * P],
                                             proj[:, k, V_COL[r] + b * DH:V_COL[r] + (b + 1) * DH],
                                             probsT[:, r, k * P:(k + 1) * P], start=False, stop=False, skip_group_check=True)
                m.then_inc(n_pv, 1)

            def nsa(i, first):
                queries_T(i, 0, n_qhat, n_qT, n_qt)
                if not first:
                    nsa_PV(8 * i - 3, 2, 1)
                queries_T(i, 1, n_qhat, n_qT, n_qt)
                if not first:
                    nsa_T(8 * i - 2, 3, 0, False)
                for u in range(8):
                    b, q = u % 2, u // 2
                    w = P * (q + 1)
                    if u < 2:
                        pe.wait_ge(n_qT, 2 * i + b + 1)
                    if not (first and u < 2):
                        pe.wait_ge(n_p, 8 * i + u - 1)
                    for r in range(2):
                        nc.tensor.matmul(S2[b][:, r, 0:w], qT[0:AUG, b, q * P:(q + 1) * P], kT[0:AUG, 2 * r + b, 0:w],
                                         start=True, stop=False)
                        m = nc.tensor.matmul(S2[b][:, r, q * P:w], identb[:], causal[:], start=False, stop=True)
                    m.then_inc(n_s, 1)
                    if u == 1:
                        for c2 in range(2):
                            for k in range(TT):
                                m = nc.tensor.matmul(banks[7][:, c2 * P + k * NC:c2 * P + (k + 1) * NC], qT[0:AUG, c2, k * P:(k + 1) * P],
                                                     kcT[0:AUG, c2, :], start=True, stop=True)
                        m.then_inc(n_sc, 1)
                    if u == 3:
                        clear_out(n_o, i, first)
                    if not (first and u < 3 or u == 0):
                        nsa_PV(8 * i + u - 3, (u - 3) % 8 // 2, (u - 3) % 2)
                    if not (first and u < 2 or u == 0):
                        nsa_T(8 * i + u - 2, (u - 2) % 8 // 2, b, first and u == 2)
                    if u >= 6:
                        pe.wait_ge(n_pcT, 2 * i + u - 5)
                        nc.tensor.matmul(banks[6][(u - 6) * DH:(u - 5) * DH, :], vc[:, u - 6, :], pcT[:, :], start=False, stop=False,
                                         skip_group_check=True)
                    if u in (5, 6):
                        pe.wait_ge(n_ew, i + 1)
                        for k in range(TT):
                            m = nc.tensor.transpose(banks[7][0:NC, k * P:(k + 1) * P], ecm[:, u - 5, k, :], ident[:])
                        m.then_inc(n_pct, 1)

            nsa(0, True)
            REST(pe, nsa)
            nsa_PV(29, 2, 1)
            nsa_T(30, 3, 0, False)
            nsa_PV(30, 3, 0)
            nsa_T(31, 3, 1, False)
            nsa_PV(31, 3, 1)

            def swa_T(i, u, first):
                v = (u - 2) % 4
                pe.wait_ge(w_w, 4 * i + u - 1)
                if not first:
                    pe.wait_ge(w_pT_v if v % 2 == 0 else w_pT_a, 2 * i + (u - 2) // 2)
                for k in range(1 if v < 2 else 0, 4):
                    m = nc.tensor.transpose(banks[4 + v % 2][:, k * P:(k + 1) * P], probs[:, v, k * P:(k + 1) * P], ident[:])
                m.then_inc(w_pt, 1)

            def swa_PV(i, u):
                v = (u - 3) % 4
                b, p = v % 2, v // 2
                pe.wait_ge(w_pT_v if v % 2 == 0 else w_pT_a, 2 * i + (u - 3) // 2 + 1)
                for q in (2 * p, 2 * p + 1):
                    for k in (([q - 1] if q > 0 else []) + [q]):
                        j = 2 * (q % 2) + (k - q + 1)
                        m = nc.tensor.matmul(banks[6][b * DH:(b + 1) * DH, q * P:(q + 1) * P],
                                             proj[:, k, C_VS + b * DH:C_VS + (b + 1) * DH], probsT[:, b, j * P:(j + 1) * P],
                                             start=False, stop=False, skip_group_check=True)
                m.then_inc(w_pv, 1)

            def swa(i, first):
                queries_T(i, 0, w_qhat, w_qT, w_qt)
                if not first:
                    swa_PV(i, 0)
                queries_T(i, 1, w_qhat, w_qT, w_qt)
                if not first:
                    swa_T(i, 0, False)
                for u in range(4):
                    b, p = u % 2, u // 2
                    if u < 2:
                        pe.wait_ge(w_qT, 2 * i + b + 1)
                    if not first:
                        pe.wait_ge(w_p, 4 * i + u - 3)
                    S = banks[u]
                    for q in (2 * p, 2 * p + 1):
                        o = (q % 2) * 2 * P
                        if q == 0:
                            nc.tensor.matmul(S[:, 0:P], identb[:], allmask[:], start=True, stop=True)
                            nc.tensor.matmul(S[:, P:2 * P], qT[0:AUG, b, 0:P], kT[0:AUG, 4 + b, 0:P], start=True, stop=False)
                        else:
                            nc.tensor.matmul(S[:, o:o + 2 * P], qT[0:AUG, b, q * P:(q + 1) * P],
                                             kT[0:AUG, 4 + b, (q - 1) * P:(q + 1) * P], start=True, stop=False)
                            nc.tensor.matmul(S[:, o:o + P], identb[:], before[:], start=False, stop=False)
                        m = nc.tensor.matmul(S[:, o + P:o + 2 * P], identb[:], causal[:], start=False, stop=True)
                    m.then_inc(w_s, 1)
                    if u == 3:
                        if first:
                            pe.wait_ge(n_o, GQ)
                        clear_out(w_o, i, first)
                    if u == 3 or (u > 0 and not first):
                        swa_PV(i, u)
                    if u >= 2 or (u > 0 and not first):
                        swa_T(i, u, first)

            pe.wait_ge(n_p, 8 * GQ)
            swa(0, True)
            REST(pe, swa)
            swa_PV(4, 0)
            swa_T(4, 0, False)
            swa_PV(4, 1)
            swa_T(4, 1, False)
            swa_PV(4, 2)

            pe.wait_ge(s_wo, 64)
            pe.wait_ge(w_p, 16)
            pe.wait_ge(n_o, GQ)

            def half_project(j, g):
                i, h = j // 2, slice((j % 2) * 512, (j % 2 + 1) * 512)
                for k in range(4):
                    m = nc.tensor.matmul(banks[2 * (j % 2) + g], featT[:, 4 * g + k, i * P:(i + 1) * P], w_out_sb[:, 4 * g + k, h],
                                         start=(k == 0), stop=(k == 3))
                return m

            def out_project(j):
                pe.wait_ge(o_x, j - 1)
                half_project(j, 0)
                half_project(j, 1).then_inc(o_pj, 1)

            half_project(0, 0)
            half_project(1, 0)
            pe.wait_ge(o_sq, 6)
            pe.wait_ge(w_qT, 2 * GQ)
            for g in range(2):
                for i in range(TT):
                    m = nc.tensor.matmul(banks[7][:, g * TT + i:g * TT + i + 1], squares[:, 4 * g, i * P:(i + 1) * P], ones[:, 0:1],
                                         start=True, stop=True)
            m.then_inc(o_ssq, 1)
            pe.wait_ge(w_o, GQ)
            for j in range(2):
                half_project(j, 1).then_inc(o_pj, 1)

            def x_hat_T(i):
                pe.wait_ge(r_xh, i + 1)
                if i == 1:
                    pe.wait_ge(o_ms, 1)
                if i >= 2:
                    pe.wait_ge(r_ev_a, i - 1)
                    pe.wait_ge(r_ev_v, i - 1)
                for k in range(KD):
                    m = nc.tensor.transpose(banks[4 + 2 * (i % 2) + k // 4][:, (k % 4) * P:(k % 4 + 1) * P], norm_x[:, i, k * P:(k + 1) * P],
                                            ident[:])
                m.then_inc(r_tr, 1)

            def logits(i):
                pe.wait_ge(r_ev_a, i + 1)
                pe.wait_ge(r_ev_v, i + 1)
                for k in range(KD):
                    m = nc.tensor.matmul(banks[0][:, i * NE:(i + 1) * NE], featT[:, k, i * P:(i + 1) * P], wr[:, k, :],
                                         start=(k == 0), stop=(k == KD - 1))
                m.then_inc(r_lg, 1)

            for j in range(2, 2 * TT):
                out_project(j)
                if j % 2 == 1 and j >= 5:
                    x_hat_T((j - 5) // 2)
            pe.wait_ge(s_wr, 16)
            pe.wait_ge(o_x, 2 * TT)
            logits(0)
            x_hat_T(2)
            logits(1)
            x_hat_T(3)
            logits(2)
            logits(3)

            pe.wait_ge(r_cnt, 1)
            pe.wait_ge(t_const, 2)
            for i in range(TT + 1):
                o = slice(i * NE, (i + 1) * NE)
                for j in range(i):
                    m = nc.tensor.matmul(banks[1][:, o], ones_b[:], mcount[:, j * NE:(j + 1) * NE], start=(j == 0),
                                         stop=(i == TT and j == TT - 1))
                if i < TT:
                    m = nc.tensor.matmul(banks[1][:, o], tri_b[:], mcount[:, o], start=(i == 0), stop=True)
            m.then_inc(r_rank, 1)

            def xg_T(g):
                pe.wait_ge(s_xg, g * 16 + 16)
                for k in range(KD):
                    m = nc.tensor.transpose(banks[4 + k // 4][:, (k % 4) * P:(k % 4 + 1) * P], xg[:, k * P:(k + 1) * P], ident[:])
                m.then_inc(m_xt, 1)

            def expert(e, b, n):
                w1, w3, w2 = exp_w[b]
                with pe.Fori(*blocks_of(pe, e)) as g:
                    pe.wait_ge(e_w[b], n * 48 + 48)
                    pe.wait_ge(m_xa, g + 1)
                    pe.wait_ge(m_xv, g + 1)
                    for m, (w, done) in enumerate(((w1, m_h1), (w3, m_h3))):
                        for k in range(KD):
                            mm = nc.tensor.matmul(banks[m], xgT[:, k, :], w[:, k, :], start=(k == 0), stop=(k == KD - 1))
                        mm.then_inc(done, 1)
                    xg_T(g + 1)
                    for q in range(2):
                        pe.wait_ge(m_h, g * 2 + (q + 1))
                        for f in range(2):
                            o = (2 * q + f) * P
                            mm = nc.tensor.transpose(banks[6 + q][:, f * P:(f + 1) * P], hmid[:, o:o + P], ident[:])
                        mm.then_inc(m_ht, 1)
                    for n in range(2):
                        for f in range(DE // P):
                            if n == 0 and f % 2 == 0:
                                pe.wait_ge(m_hT, g * 2 + (f // 2 + 1))
                            mm = nc.tensor.matmul(banks[2 + n], hT[:, f, :], w2[:, f, n * 512:(n + 1) * 512], start=(f == 0),
                                                  stop=(f == DE // P - 1))
                        mm.then_inc(m_y, 1)

            xg_T(0)
            pe.wait_ge(t_gs, 1)
            with pe.Fori(0, NE // 2) as n:
                for b in range(2):
                    expert(n * 2 + b, b, n)


_INS = ['x', 'c', 'w_router', 'ada_w', 'ada_b', 'norm1_g', 'norm2_g', 'w_in', 'w_out', 'nsa_q_gain', 'nsa_k_gain',
        'cmp_pos_k', 'cmp_pos_v', 'cmp_w1_k', 'cmp_w2_k', 'cmp_w1_v', 'cmp_w2_v', 'swa_q_gain', 'swa_k_gain',
        'swa_sinks', 'beta_nsa', 'beta_swa', 'moe_w1', 'moe_w3', 'moe_w2']


def kernel(**inputs):
    import numpy as _np
    import concourse.bacc as _bacc
    from concourse import mybir as _mybir
    from concourse.bass_utils import run_bass_kernel_spmd as _run

    nc = _bacc.Bacc("TRN2", target_bir_lowering=False, num_devices=1)
    arrays, args = {}, []
    for name in _INS:
        a = _np.ascontiguousarray(inputs[name])
        arrays[f"in_{name}"] = a
        args.append(nc.dram_tensor(f"in_{name}", a.shape, _mybir.dt.from_np(a.dtype), kind="ExternalInput").ap())
    args.append(nc.dram_tensor("out_dram", (1, T, D), F32, kind="ExternalOutput").ap())
    decoder_layer(nc, *args)
    r = _run(nc, [arrays], core_ids=[0])
    return r.results[0]["out_dram"]
```
